# Optimizing a Trainium2 kernel written in Bass

```python
import math
import jax, jax.numpy as jnp
from jax import lax
import numpy as np

D_MODEL = 2048
BATCH = 1
SEQ = 256
DEPTH = 2

N_MIXERS = 2
A_HEAD_DIM = 128
A_HEADS = D_MODEL // (2 * A_HEAD_DIM)
A_V_DIM = 2 * A_HEAD_DIM
A_QK = A_HEADS * 2 * A_HEAD_DIM
A_WIDTH = A_HEADS * A_V_DIM
A_IN = 2 * A_QK + 2 * A_WIDTH
B_GROUPS = ((128, 1), (512, 4), (2048, 16))
B_HEAD_DIM = 128
B_HEADS = D_MODEL // B_HEAD_DIM
B_WIDTH = B_HEADS * B_HEAD_DIM
B_IN = 3 * len(B_GROUPS) * B_WIDTH + B_WIDTH
Q_BLOCK = 128
RMS_EPS = 1e-6

kernel_name = "hybrid_diffattn_dilated_gated"

def rms_norm(x, g):
    xf = x.astype(jnp.float32)
    y = xf * lax.rsqrt(jnp.mean(xf * xf, axis=-1, keepdims=True) + RMS_EPS)
    return (y * g.astype(jnp.float32)).astype(x.dtype)

def alibi_slopes(n):
    return jnp.exp2(-8.0 * (jnp.arange(n, dtype=jnp.float32) + 1.0) / n)

def lambda_init_fn(layer_idx):
    return 0.8 - 0.6 * math.exp(-0.3 * layer_idx)

def diff_attention(q1, q2, k1, k2, v, lam):
    b, s, h, d = q1.shape
    nblk = s // Q_BLOCK
    slopes = alibi_slopes(h)
    kpos = jnp.arange(s)
    scale = d ** -0.5

    def one_block(args):
        qa, qb, i = args
        qpos = i * Q_BLOCK + jnp.arange(Q_BLOCK)
        dist = qpos[:, None] - kpos[None, :]
        bias = -slopes[:, None, None] * dist.astype(jnp.float32)
        causal = dist >= 0
        s1 = jnp.einsum('bqhd,bshd->bhqs', qa, k1).astype(jnp.float32) * scale + bias
        s2 = jnp.einsum('bqhd,bshd->bhqs', qb, k2).astype(jnp.float32) * scale + bias
        p1 = jax.nn.softmax(jnp.where(causal, s1, -jnp.inf), axis=-1)
        p2 = jax.nn.softmax(jnp.where(causal, s2, -jnp.inf), axis=-1)
        p = (p1 - lam * p2).astype(v.dtype)
        return jnp.einsum('bhqs,bshe->bqhe', p, v)

    def to_blocks(t):
        return t.reshape(b, nblk, Q_BLOCK, h, d).transpose(1, 0, 2, 3, 4)

    out = lax.map(one_block, (to_blocks(q1), to_blocks(q2), jnp.arange(nblk)))
    return out.transpose(1, 0, 2, 3, 4).reshape(b, s, h, 2 * d)

def dilated_group(q, k, v, window, dilation, slopes):
    b, s, h, dh = q.shape
    w = window // dilation
    L = s // dilation
    nblk = -(-L // w)
    Lp = nblk * w
    scale = dh ** -0.5

    def split(t):
        t = t.reshape(b, L, dilation, h, dh).transpose(0, 2, 1, 3, 4)
        return jnp.pad(t, ((0, 0), (0, 0), (0, Lp - L), (0, 0), (0, 0)))

    def band(t):
        tb = t.reshape(b, dilation, nblk, w, h, dh)
        prev = jnp.pad(tb, ((0, 0), (0, 0), (1, 0), (0, 0), (0, 0), (0, 0)))[:, :, :-1]
        return jnp.concatenate([prev, tb], axis=3)

    qb = split(q).reshape(b, dilation, nblk, w, h, dh)
    kb = band(split(k))
    vb = band(split(v))
    rel = (jnp.arange(w)[:, None] + w) - jnp.arange(2 * w)[None, :]
    key_sub = jnp.arange(nblk)[:, None] * w - w + jnp.arange(2 * w)[None, :]
    valid = ((rel >= 0) & (rel <= w))[None] & (key_sub >= 0)[:, None, :]
    bias = -slopes[:, None, None] * (rel * dilation).astype(jnp.float32)
    sc = jnp.einsum('brnqhd,brnkhd->brnhqk', qb, kb).astype(jnp.float32) * scale + bias
    sc = jnp.where(valid[:, None], sc, -jnp.inf)
    m = jnp.max(sc, axis=-1, keepdims=True)
    p = jnp.exp(sc - m)
    den = jnp.sum(p, axis=-1, keepdims=True)
    out = jnp.einsum('brnhqk,brnkhd->brnqhd', (p / den).astype(v.dtype), vb)
    lse = (m + jnp.log(den))[..., 0]
    out = out.reshape(b, dilation, Lp, h, dh)[:, :, :L].transpose(0, 2, 1, 3, 4).reshape(b, s, h, dh)
    lse = lse.transpose(0, 1, 2, 4, 3).reshape(b, dilation, Lp, h)[:, :, :L]
    lse = lse.transpose(0, 2, 1, 3).reshape(b, s, h)
    return out, lse

def mixer_a(hn, w_in, lam_q1, lam_k1, lam_q2, lam_k2, subln, w_out, lam_init):
    b, s, _ = hn.shape
    proj = hn @ w_in
    q, k, v, z = jnp.split(proj, [A_QK, 2 * A_QK, 2 * A_QK + A_WIDTH], axis=-1)
    q = q.reshape(b, s, A_HEADS, 2, A_HEAD_DIM)
    k = k.reshape(b, s, A_HEADS, 2, A_HEAD_DIM)
    v = v.reshape(b, s, A_HEADS, A_V_DIM)
    f32 = jnp.float32
    lam = (jnp.exp(jnp.sum(lam_q1.astype(f32) * lam_k1.astype(f32)))
           - jnp.exp(jnp.sum(lam_q2.astype(f32) * lam_k2.astype(f32))) + lam_init)
    o = diff_attention(q[:, :, :, 0], q[:, :, :, 1], k[:, :, :, 0], k[:, :, :, 1], v, lam)
    o = rms_norm(o, subln) * (1.0 - lam_init)
    o = o.reshape(b, s, A_WIDTH) * jax.nn.silu(z)
    return o @ w_out

def mixer_b(hn, w_in, w_out):
    b, s, _ = hn.shape
    n_g = len(B_GROUPS)
    proj = hn @ w_in
    qkv = proj[..., :3 * n_g * B_WIDTH].reshape(b, s, n_g, 3, B_HEADS, B_HEAD_DIM)
    z = proj[..., 3 * n_g * B_WIDTH:]
    slopes = alibi_slopes(B_HEADS)
    outs, lses = [], []
    for g, (window, dil) in enumerate(B_GROUPS):
        o, l = dilated_group(qkv[:, :, g, 0], qkv[:, :, g, 1], qkv[:, :, g, 2], window, dil, slopes)
        outs.append(o)
        lses.append(l)
    alpha = jax.nn.softmax(jnp.stack(lses, axis=0), axis=0)
    o = jnp.sum(alpha[..., None].astype(hn.dtype) * jnp.stack(outs, axis=0), axis=0)
    o = o.reshape(b, s, B_WIDTH) * jax.nn.silu(z)
    return o @ w_out

def setup_inputs(seed: int = 0) -> dict:
    key = jax.random.key(seed)
    ks = jax.random.split(key, 13)
    n_a = (DEPTH + 1) // 2
    n_b = DEPTH // 2
    nrm = jax.random.normal
    f32 = jnp.float32
    return {
        "x": nrm(ks[0], (BATCH, SEQ, D_MODEL), f32),
        "norm_a": 1.0 + 0.1 * nrm(ks[1], (n_a, D_MODEL), f32),
        "w_in_a": nrm(ks[2], (n_a, D_MODEL, A_IN), f32) * D_MODEL ** -0.5,
        "lam_q1": 0.1 * nrm(ks[3], (n_a, A_HEAD_DIM), f32),
        "lam_k1": 0.1 * nrm(ks[4], (n_a, A_HEAD_DIM), f32),
        "lam_q2": 0.1 * nrm(ks[5], (n_a, A_HEAD_DIM), f32),
        "lam_k2": 0.1 * nrm(ks[6], (n_a, A_HEAD_DIM), f32),
        "subln_a": 1.0 + 0.1 * nrm(ks[7], (n_a, A_V_DIM), f32),
        "w_out_a": nrm(ks[8], (n_a, A_WIDTH, D_MODEL), f32) * A_WIDTH ** -0.5,
        "norm_b": 1.0 + 0.1 * nrm(ks[9], (n_b, D_MODEL), f32),
        "w_in_b": nrm(ks[10], (n_b, D_MODEL, B_IN), f32) * D_MODEL ** -0.5,
        "w_out_b": nrm(ks[11], (n_b, B_WIDTH, D_MODEL), f32) * B_WIDTH ** -0.5,
        "norm_f": 1.0 + 0.1 * nrm(ks[12], (D_MODEL,), f32),
    }

def reference(x, norm_a, w_in_a, lam_q1, lam_k1, lam_q2, lam_k2, subln_a, w_out_a,
              norm_b, w_in_b, w_out_b, norm_f):
    h = x
    for i in range(DEPTH):
        j = i // N_MIXERS
        if i % N_MIXERS == 0:
            y = mixer_a(rms_norm(h, norm_a[j]), w_in_a[j], lam_q1[j], lam_k1[j], lam_q2[j],
                        lam_k2[j], subln_a[j], w_out_a[j], lambda_init_fn(i))
        else:
            y = mixer_b(rms_norm(h, norm_b[j]), w_in_b[j], w_out_b[j])
        h = h + y
    return rms_norm(h, norm_f)


_drawn_inputs = setup_inputs


def setup_inputs(seed=0):
    import zlib

    import numpy as np

    out = dict(_drawn_inputs(seed))
    spreads = {}
    factors = {'lam_q1': 2.953}
    for name, (base, spread) in spreads.items():
        noise = np.random.default_rng([zlib.crc32(name.encode()), seed]).standard_normal(out[name].shape)
        drawn = base * np.exp(spread * noise) if base else spread * noise
        out[name] = __import__('jax').numpy.asarray(drawn.astype(out[name].dtype))
    for name, factor in factors.items():
        out[name] = (out[name] * factor).astype(out[name].dtype)
    return out
```

```python
from contextlib import ExitStack
import math

import numpy as np

import concourse.bass as bass
from concourse import mybir
from concourse.alu_op_type import AluOpType as ALU

F32 = mybir.dt.float32
F32R = mybir.dt.float32r
ACT = mybir.ActivationFunctionType
AX = mybir.AxisListType

P = 128
D_MODEL = 2048
SEQ = 256
TOK = SEQ // P
KT = D_MODEL // P
COLS = 512
PIECE_KT = 2
PIECES = KT // PIECE_KT
RING = 4
OUT_CHUNKS = D_MODEL // COLS
HEAD = 128
SCALE = HEAD ** -0.5
RMS_EPS = 1e-6
A_HEADS = 8
A_VDIM = 256
A_ITER = 4
A_CHUNKS = 4
B_HEADS = 16
B_GROUPS = ((128, 1), (512, 4), (2048, 16))
NG = len(B_GROUPS)
B_ITER = 4
B_CHUNKS = 3 * NG + 1
B_HPI = B_HEADS // B_ITER
SPAN = P + SEQ
LAM_INIT = 0.8 - 0.6 * math.exp(0.0)
MASKED = -1.0e30

PIECES_A = A_CHUNKS * PIECES
PIECES_B = B_CHUNKS * PIECES
OUT_A = A_ITER * PIECES_A
LAYER_B = OUT_A + OUT_CHUNKS * PIECES
OUT_B = LAYER_B + B_ITER * PIECES_B
ALL_PIECES = OUT_B + OUT_CHUNKS * PIECES

A_TR, B_TR = 6, 24
A_NAT, B_NAT = 3, 3 * NG
A_QK, B_QK = 4, NG * B_HPI
A_PV, B_PV = 2, B_HPI
A_STEPS, B_STEPS = 10, 9

P_TURNS = {(7, 4): 0, (7, 5): 2, (7, 6): 4, (7, 7): 6, (8, 1): 8, (8, 2): 10}
O_TURNS = {0: (2,), 1: (3,), 2: (4,), 3: (5,), 5: (6, 7)}


class Links:

    def __init__(self, eng, sem):
        self.eng, self.sem, self.n, self.base = eng, sem, 0, 0

    def link(self, ins):
        self.n += 1
        ins.then_inc(self.sem, 1)
        self.eng.wait_ge(self.sem, self.base + self.n)


def hybrid(nc, x, w_in_a, w_out_a, w_in_b, w_out_b, norm_a, norm_b, norm_f, subln, lams, dist,
           slopes, ident, out):
    with ExitStack() as ctx:
        def sem(name):
            return ctx.enter_context(nc.semaphore(name))

        start = (nc.sbuf_base + 31) // 32 * 32
        total = [0]
        places = []

        def place(name, shape, dt, at=None):
            size = 4 * int(np.prod(shape[1:]))
            offset = total[0] if at is None else at
            if at is None:
                total[0] += (size + 31) // 32 * 32
            places.append((name, shape, dt, offset))
            return offset + size

        place("raw", [P, RING, PIECE_KT * COLS], F32)
        place("w_hi", [P, RING, PIECE_KT * COLS], F32R)
        place("w_lo", [P, RING, PIECE_KT * COLS], F32R)
        first = total[0]
        place("xa_hi", [P, KT, SEQ], F32R)
        place("xa_lo", [P, KT, SEQ], F32R)
        place("oa_hi", [P, KT, SEQ], F32R, first)
        place("oa_lo", [P, KT, SEQ], F32R, first + 4 * KT * SEQ)
        after = place("ob_nat", [P, TOK, D_MODEL], F32, first)
        place("v_b", [P, NG, TOK, COLS], F32, after)
        second = total[0]
        place("xb_hi", [P, KT, SEQ], F32R)
        place("xb_lo", [P, KT, SEQ], F32R)
        place("ob_hi", [P, KT, SEQ], F32R, second)
        place("ob_lo", [P, KT, SEQ], F32R, second + 4 * KT * SEQ)
        after = place("oa_nat", [P, TOK, D_MODEL], F32, second)
        after = place("v_a", [P, 1, TOK, COLS], F32, after)
        after = place("t_a", [P, 4, SPAN], F32, after)
        place("p_a", [P, 2, SPAN], F32, after)
        place("h", [P, TOK, D_MODEL], F32)
        place("nat", [P, TOK, COLS], F32)
        place("q_t", [P, 4, SEQ], F32)
        place("k_t", [P, 4, SEQ], F32)
        third = total[0]
        place("t_b", [P, B_HPI, NG, SPAN], F32)
        place("pt_b", [P, B_HPI * NG, SPAN], F32)
        place("pt_a", [P, 2, SPAN], F32, third)
        after = place("normf_sb", [P, D_MODEL], F32, third)
        place("final", [P, TOK, D_MODEL], F32, after)
        place("og", [P, TOK, COLS], F32)
        place("e", [P, TOK, COLS], F32)
        place("squares", [P, TOK, COLS], F32)
        place("dist_sb", [P, 1 + NG, SPAN], F32)
        place("ident_sb", [P, P], F32)
        place("slopes_sb", [P, A_HEADS + B_HEADS], F32)
        place("norm_a_sb", [P, KT], F32)
        place("norm_b_sb", [P, KT], F32)
        place("subln_sb", [P, A_VDIM], F32)
        place("lams_sb", [P, 4, HEAD], F32)
        place("lam_prod", [P, 2, HEAD], F32)
        place("lam", [P, 8], F32)
        place("nm", [P, 2, 4], F32)
        place("den", [P, 2, 4], F32)
        place("rden", [P, 2, 4], F32)
        place("ssq", [P, TOK, OUT_CHUNKS], F32)
        place("ssq2", [P, 2, TOK], F32)
        place("ms", [P, 2, 8], F32)
        place("rstd", [P, 3, TOK], F32)
        place("nrstd", [P, 2, TOK], F32)
        place("rstd2", [P, 2, TOK], F32)
        place("consts", [P, 4, 8], F32)
        ctx.enter_context(nc.sbuf_tensor("arena", [P, total[0] // 4 + 8], F32))
        sb = {name: nc.alloc_sbuf_tensor_at(name, shape, dt, offset=start + offset)
              for name, shape, dt, offset in places}
        raw, w_hi, w_lo, h, nat = (sb[n] for n in ("raw", "w_hi", "w_lo", "h", "nat"))
        q_t, k_t, og, e = (sb[n] for n in ("q_t", "k_t", "og", "e"))
        squares, dist_sb, ident_sb, slopes_sb = (
            sb[n] for n in ("squares", "dist_sb", "ident_sb", "slopes_sb"))
        lam, nm, den, rden, ssq, ssq2, ms, rstd, nrstd, rstd2, consts = (
            sb[n] for n in ("lam", "nm", "den", "rden", "ssq", "ssq2", "ms", "rstd", "nrstd",
                            "rstd2", "consts"))
        t_a, p_a, pt_a, t_b, pt_b = (sb[n] for n in ("t_a", "p_a", "pt_a", "t_b", "pt_b"))

        proj = ctx.enter_context(nc.psum_tensor("proj", [P, 2, TOK, COLS], F32))
        turned = ctx.enter_context(nc.psum_tensor("turned", [P, 2, COLS], F32))
        score = ctx.enter_context(nc.psum_tensor("score", [P, 2, COLS], F32))

        landed = [sem(f"landed{s}") for s in range(RING)]
        x_landed = [sem(f"x_landed{c}") for c in range(OUT_CHUNKS)]
        const_landed = sem("const_landed")
        normf_landed = sem("normf_landed")
        hi_done = sem("hi_done")
        lo_done = sem("lo_done")
        pe_used = sem("pe_used")
        xt_turned = sem("xt_turned")
        xt_hi = sem("xt_hi")
        xt_lo = sem("xt_lo")
        ot_turned = sem("ot_turned")
        ot_hi = sem("ot_hi")
        ot_lo = sem("ot_lo")
        tr_turned = sem("tr_turned")
        tr_copied = sem("tr_copied")
        nat_ready = sem("nat_ready")
        qk_done = sem("qk_done")
        t_ready = sem("t_ready")
        max_ready = sem("max_ready")
        exp_done = sem("exp_done")
        p_ready = sem("p_ready")
        pv_done = sem("pv_done")
        pv_out = sem("pv_out")
        ssq2_done = sem("ssq2_done")
        rstd2_done = sem("rstd2_done")
        z_exp = sem("z_exp")
        o_ready = sem("o_ready")
        h_ready = sem("h_ready")
        ssq_done = sem("ssq_done")
        ms_done = sem("ms_done")
        rstd_done = sem("rstd_done")
        lam_dot = sem("lam_dot")
        lam_exp = sem("lam_exp")
        dve_link = sem("dve_link")
        pool_link = sem("pool_link")
        pre_done = sem("pre_done")
        final_act = sem("final_act")
        final_dve = sem("final_dve")
        stored = sem("stored")

        w_a = w_in_a.rearrange("(t p) n -> p t n", p=P)
        w_b = w_in_b.rearrange("(t p) n -> p t n", p=P)
        wo_a = w_out_a.rearrange("(t p) n -> p t n", p=P)
        wo_b = w_out_b.rearrange("(t p) n -> p t n", p=P)
        x_v = x.rearrange("(b p) n -> p b n", p=P)
        out_v = out.rearrange("(b p) n -> p b n", p=P)

        b_first = [(3 * g + s) * D_MODEL for g in range(NG) for s in (0, 1)]
        b_first += [(3 * g + 2) * D_MODEL for g in range(NG)] + [3 * NG * D_MODEL]
        V_B, Z_B = 2 * NG, B_CHUNKS - 1

        block = ctx.enter_context(nc.Block())

        @block.sync
        def _(sp):
            def piece(view, col, n0, c, j):
                if not isinstance(n0, int) or n0 + c * PIECES + j >= RING:
                    sp.wait_ge(lo_done, n0 + (c * PIECES + j - RING + 1))
                sp.dma_start(raw[:, j % RING].rearrange("p (t n) -> p t n", t=PIECE_KT),
                             view[:, PIECE_KT * j:PIECE_KT * (j + 1), col]
                             ).then_inc(landed[j % RING], 16)

            def columns(start):
                return bass.ds(start, COLS)

            sp.dma_start(ident_sb[:, :], ident).then_inc(const_landed, 16)
            sp.dma_start(sb["norm_a_sb"][:, :], norm_a).then_inc(const_landed, 16)
            for c in range(OUT_CHUNKS):
                sp.dma_start(h[:, :, COLS * c:COLS * (c + 1)],
                             x_v[:, :, COLS * c:COLS * (c + 1)]).then_inc(x_landed[c], 16)
                piece(w_a, slice(0, COLS), 0, 0, c)
            for to, of in ((sb["norm_b_sb"][:, :], norm_b), (slopes_sb[:, :], slopes),
                           (sb["subln_sb"][:, :], subln),
                           (sb["lams_sb"][:, :, :].rearrange("p a b -> p (a b)"), lams),
                           (dist_sb[:, :, :].rearrange("p a b -> p (a b)"), dist)):
                sp.dma_start(to, of).then_inc(const_landed, 16)
            for c in range(A_CHUNKS):
                for j in range(PIECES):
                    if c * PIECES + j >= RING:
                        piece(w_a, slice(c * D_MODEL, c * D_MODEL + COLS), 0, c, j)
            with sp.Fori(1, A_ITER) as i:
                for c in range(A_CHUNKS):
                    for j in range(PIECES):
                        piece(w_a, columns(i * COLS + c * D_MODEL), i * PIECES_A, c, j)
            for c in range(OUT_CHUNKS):
                for j in range(PIECES):
                    piece(wo_a, slice(c * COLS, c * COLS + COLS), OUT_A, c, j)
            with sp.Fori(0, B_ITER) as i:
                for c in range(B_CHUNKS):
                    for j in range(PIECES):
                        piece(w_b, columns(i * COLS + b_first[c]), i * PIECES_B + LAYER_B, c, j)
            sp.wait_ge(tr_copied, A_ITER * A_TR + B_ITER * B_TR)
            sp.dma_start(sb["normf_sb"][:, :], norm_f).then_inc(normf_landed, 16)
            for c in range(OUT_CHUNKS):
                for j in range(PIECES):
                    piece(wo_b, slice(c * COLS, c * COLS + COLS), OUT_B, c, j)
            half_cols = D_MODEL // 2
            for n in range(2):
                cut = slice(half_cols * n, half_cols * (n + 1))
                sp.wait_ge(final_act, n + 1)
                sp.dma_start(out_v[:, 0, cut], sb["final"][:, 0, cut]).then_inc(stored, 16)
                sp.wait_ge(final_dve, n + 1)
                sp.dma_start(out_v[:, 1, cut], sb["final"][:, 1, cut]).then_inc(stored, 16)
            sp.wait_ge(stored, 4 * 16)

        @block.tensor
        def _(pe):
            def turn(bank, at, of):
                return pe.matmul(turned[:, bank, at:at + P], of, ident_sb[:, :],
                                 start=True, stop=True, is_transpose=True)

            def matmuls(lhs_hi, lhs_lo, c, j):
                s = j % RING
                for k in range(PIECE_KT):
                    kt = PIECE_KT * j + k
                    cut = slice(COLS * k, COLS * (k + 1))
                    for b in range(TOK):
                        tok = slice(P * b, P * (b + 1))
                        to = proj[:, c % 2, b, :]
                        pe.matmul(to, lhs_hi[:, kt, tok], w_hi[:, s, cut], start=(kt == 0),
                                  stop=False)
                        pe.matmul(to, lhs_hi[:, kt, tok], w_lo[:, s, cut], start=False, stop=False)
                        last = pe.matmul(to, lhs_lo[:, kt, tok], w_hi[:, s, cut], start=False,
                                         stop=(kt == KT - 1))
                last.then_inc(pe_used, 1)

            def turn_x(c, half_c, n):
                for k in range(2):
                    for b in range(TOK):
                        col = COLS * c + P * (2 * half_c + k)
                        last = turn(n % 2, SEQ * k + P * b, h[:, b, col:col + P])
                last.then_inc(xt_turned, 1)

            def turn_nat(first_block, bank):
                for k in range(2):
                    for b in range(TOK):
                        col = P * (first_block + k)
                        last = turn(bank, SEQ * k + P * b, nat[:, b, col:col + P])
                last.then_inc(tr_turned, 1)

            def scores(block_n, bank):
                pe.matmul(score[:, bank, 0:P], q_t[:, block_n, 0:P], k_t[:, block_n, 0:P],
                          start=True, stop=True)
                pe.matmul(score[:, bank, P:SPAN], q_t[:, block_n, P:SEQ], k_t[:, block_n, :],
                          start=True, stop=True).then_inc(qk_done, 1)

            def turn_p(of, bank):
                for n in range(3):
                    last = turn(bank, P * n, of[:, P * n:P * (n + 1)])
                last.then_inc(tr_turned, 1)

            pe.wait_ge(const_landed, 32)
            for n in range(2 * OUT_CHUNKS):
                pe.wait_ge(x_landed[n // 2], 16)
                if n >= 2:
                    pe.wait_ge(xt_lo, n - 1)
                turn_x(n // 2, n % 2, n)

            with pe.Fori(0, A_ITER) as i:
                for c in range(A_CHUNKS):
                    for j in range(PIECES):
                        if c in (1, 2) and j in (1, 2):
                            if j == 1:
                                pe.wait_ge(nat_ready, i * A_NAT + c)
                            if c == 2:
                                pe.wait_ge(tr_copied, i * A_TR + j)
                            turn_nat(2 * (j - 1), j - 1)
                        if c == 2 and j in (4, 6):
                            pe.wait_ge(tr_copied, i * A_TR + 4)
                            if j == 6:
                                pe.wait_ge(t_ready, i * A_QK + 2)
                            for n in range(2):
                                scores(j - 4 + n, n)
                        if c == 3 and j == 4:
                            pe.wait_ge(p_ready, i + 1)
                            for n in range(2):
                                turn_p(p_a[:, n], n)
                        if c == 3 and j == 5:
                            pe.wait_ge(tr_copied, i * A_TR + A_TR)
                            pe.wait_ge(nat_ready, i * A_NAT + A_NAT)
                            for n in range(2):
                                v = sb["v_a"][:, 0, :, A_VDIM * n:A_VDIM * (n + 1)]
                                pe.matmul(score[:, n, 0:A_VDIM], pt_a[:, n, 0:P], v[:, 0],
                                          start=True, stop=True)
                                pe.matmul(score[:, n, A_VDIM:], pt_a[:, n, P:2 * P], v[:, 0],
                                          start=True, stop=False)
                                pe.matmul(score[:, n, A_VDIM:], pt_a[:, n, 2 * P:], v[:, 1],
                                          start=False, stop=True).then_inc(pv_done, 1)
                        if c == 0:
                            pe.wait_ge(xt_lo, j + 1)
                        pe.wait_ge(lo_done, i * PIECES_A + (c * PIECES + j + 1))
                        matmuls(sb["xa_hi"], sb["xa_lo"], c, j)

            def turn_o(o_nat, n, base, o_base):
                pe.wait_ge(o_ready, o_base + n // 2 + 1)
                if n >= 2:
                    pe.wait_ge(ot_hi, base + n - 1)
                for k in range(2):
                    for b in range(TOK):
                        last = turn(n % 2, SEQ * k + P * b,
                                    o_nat[:, b, P * (2 * n + k):P * (2 * n + k + 1)])
                last.then_inc(ot_turned, 1)

            def out_projection(o_nat, o_hi, o_lo, first_piece, base, o_base, turn_h):
                for n in range(2):
                    turn_o(o_nat, n, base, o_base)
                for c in range(OUT_CHUNKS):
                    for j in range(PIECES):
                        if c == 0:
                            for n in O_TURNS.get(j, ()):
                                turn_o(o_nat, n, base, o_base)
                            pe.wait_ge(ot_lo, base + j + 1)
                        if c >= 1 and turn_h and j in (1, 2):
                            n = 2 * (c - 1) + j - 1
                            pe.wait_ge(h_ready, c)
                            if n >= 2:
                                pe.wait_ge(xt_lo, PIECES + n - 1)
                            turn_x(c - 1, j - 1, n)
                        pe.wait_ge(lo_done, first_piece + c * PIECES + j + 1)
                        matmuls(o_hi, o_lo, c, j)

            out_projection(sb["oa_nat"], sb["oa_hi"], sb["oa_lo"], OUT_A, 0, 0, True)
            pe.wait_ge(h_ready, OUT_CHUNKS)
            for n in (6, 7):
                pe.wait_ge(xt_lo, PIECES + n - 1)
                turn_x(3, n - 6, n)

            tr0, nat0, qk0 = A_ITER * A_TR, A_ITER * A_NAT, A_ITER * A_QK
            pv0 = A_ITER * A_PV
            with pe.Fori(0, B_ITER) as i:
                for c in range(B_CHUNKS):
                    for j in range(PIECES):
                        if 1 <= c <= V_B and j in (1, 2):
                            if j == 1:
                                pe.wait_ge(nat_ready, i * B_NAT + (nat0 + c))
                            if c >= 2:
                                pe.wait_ge(tr_copied, i * B_TR + (tr0 + 2 * (c - 1) + j - 2))
                            turn_nat(2 * (j - 1), j - 1)
                        if c in (2, 4, 6) and j in (4, 6):
                            pe.wait_ge(tr_copied, i * B_TR + (tr0 + 2 * c))
                            n0 = 4 * (c // 2 - 1) + (j - 4)
                            if n0 >= 2:
                                pe.wait_ge(t_ready, i * B_QK + (qk0 + n0))
                            for n in range(2):
                                scores(j - 4 + n, n)
                        m = P_TURNS.get((c, j))
                        if m is not None:
                            for n in (m, m + 1):
                                hd = n // NG
                                pe.wait_ge(exp_done, i * B_HPI + (A_ITER + hd + 1))
                                pe.wait_ge(tr_copied, i * B_TR + (tr0 + 4 * NG + n - 1))
                                turn_p(t_b[:, hd, n % NG], n % 2)
                        if c == Z_B and 1 <= j <= B_HPI:
                            hd = j - 1
                            pe.wait_ge(tr_copied, i * B_TR + (tr0 + 4 * NG + NG * (hd + 1)))
                            pe.wait_ge(nat_ready, i * B_NAT + (nat0 + B_NAT))
                            if hd >= 2:
                                pe.wait_ge(pv_out, i * B_PV + (pv0 + hd - 1))
                            v = sb["v_b"][:, :, :, HEAD * hd:HEAD * (hd + 1)]
                            for g in range(NG):
                                pe.matmul(score[:, hd % 2, 0:P], pt_b[:, NG * hd + g, 0:P],
                                          v[:, g, 0], start=(g == 0), stop=(g == NG - 1))
                            for g in range(NG):
                                for b in range(TOK):
                                    last = pe.matmul(
                                        score[:, hd % 2, P:2 * P],
                                        pt_b[:, NG * hd + g, P * (b + 1):P * (b + 2)],
                                        v[:, g, b], start=(g == 0 and b == 0),
                                        stop=(g == NG - 1 and b == TOK - 1))
                            last.then_inc(pv_done, 1)
                        if c == 0:
                            pe.wait_ge(xt_lo, PIECES + j + 1)
                        pe.wait_ge(lo_done, i * PIECES_B + (LAYER_B + c * PIECES + j + 1))
                        matmuls(sb["xb_hi"], sb["xb_lo"], c, j)

            out_projection(sb["ob_nat"], sb["ob_hi"], sb["ob_lo"], OUT_B, PIECES, A_ITER, False)

        @block.scalar
        def _(act):
            def split(n0, n):
                s = n % RING
                act.wait_ge(landed[s], n0 * (16 // RING) + 16 * (n // RING + 1))
                if not isinstance(n0, int) or n0 + n >= RING:
                    act.wait_ge(pe_used, n0 + (n - RING + 1))
                act.activation(w_hi[:, s], raw[:, s], ACT.Copy).then_inc(hi_done, 1)

            def chunk_out(to, c, scale_by):
                for b in range(TOK):
                    last = act.activation(to[:, b], proj[:, c % 2, b, :], ACT.Copy,
                                          scale=scale_by[:, b:b + 1])
                last.then_inc(nat_ready, 1)

            def copy_turned(to, bank, n, width):
                act.wait_ge(tr_turned, n)
                act.activation(to, turned[:, bank, 0:width], ACT.Copy).then_inc(tr_copied, 1)

            def x_hi(x_hi_sb, gain, n, base):
                act.wait_ge(xt_turned, base + n + 1)
                for k in range(2):
                    kt = 2 * n + k
                    last = act.activation(x_hi_sb[:, kt, :],
                                          turned[:, n % 2, SEQ * k:SEQ * (k + 1)], ACT.Copy,
                                          scale=gain[:, kt:kt + 1])
                last.then_inc(xt_hi, 1)

            def sum_squares(c):
                for b in range(TOK):
                    last = act.activation(squares[:, b], h[:, b, COLS * c:COLS * (c + 1)],
                                          ACT.Square, accum_out=ssq[:, b, c:c + 1])
                    last.then_inc(ssq_done, 1)

            def z_part(c, layer):
                for b in range(TOK):
                    act.activation(e[:, b], proj[:, c % 2, b, :], ACT.Exp,
                                   scale=nrstd[:, layer, b:b + 1]).then_inc(z_exp, 1)

            act.wait_ge(const_landed, 32)
            for c in range(OUT_CHUNKS):
                for n in (2 * c, 2 * c + 1):
                    x_hi(sb["xa_hi"], sb["norm_a_sb"], n, 0)
                split(0, c)
            for c in range(OUT_CHUNKS):
                if c:
                    act.wait_ge(ssq_done, TOK * c)
                sum_squares(c)
            act.wait_ge(lam_dot, 2)
            act.activation(lam[:, 2:4], lam[:, 0:2], ACT.Exp).then_inc(lam_exp, 1)

            act.wait_ge(rstd_done, 1)
            with act.Fori(0, A_ITER) as i:
                for c in range(A_CHUNKS):
                    for j in range(PIECES):
                        if c in (1, 2) and j in (1, 2):
                            to = (q_t, k_t)[c - 1]
                            copy_turned(to[:, 2 * (j - 1):2 * j, :], j - 1,
                                        i * A_TR + (2 * (c - 1) + j), 2 * SEQ)
                        if c == 3 and j == 0:
                            act.wait_ge(max_ready, i + 1)
                            for n in range(4):
                                for b, cut in ((0, slice(0, P)), (1, slice(P, SPAN))):
                                    last = act.activation(
                                        t_a[:, n, cut], t_a[:, n, cut], ACT.Exp, scale=SCALE,
                                        bias=nm[:, b, n:n + 1], accum_out=den[:, b, n:n + 1])
                            last.then_inc(exp_done, 1)
                        if c == 3 and j == 4:
                            for n in range(2):
                                copy_turned(pt_a[:, n, :], n, i * A_TR + 5 + n, SPAN)
                        if c == 3 and j == 6:
                            act.wait_ge(pv_out, i * A_PV + A_PV)
                            for n in range(2):
                                for b in range(TOK):
                                    last = act.activation(
                                        squares[:, b, A_VDIM * n:A_VDIM * (n + 1)],
                                        og[:, b, A_VDIM * n:A_VDIM * (n + 1)], ACT.Square,
                                        accum_out=ssq2[:, n, b:b + 1])
                                    last.then_inc(ssq2_done, 1)
                        if j == PIECES - 1:
                            act.wait_ge(pe_used, i * PIECES_A + (c + 1) * PIECES)
                            if c < 2:
                                chunk_out(nat, c, rstd[:, 0])
                            elif c == 2:
                                chunk_out(sb["v_a"][:, 0], c, rstd[:, 0])
                            else:
                                z_part(c, 0)
                        split(i * PIECES_A, c * PIECES + j + RING)

            def o_hi_parts(o_hi, n, base):
                act.wait_ge(ot_turned, base + n + 1)
                if n >= 2:
                    act.wait_ge(ot_lo, base + n - 1)
                act.activation(nat[:, n % 2, :], turned[:, n % 2, :], ACT.Copy)
                act.activation(o_hi[:, 2 * n:2 * n + 2, :], turned[:, n % 2, :],
                               ACT.Copy).then_inc(ot_hi, 1)

            def out_projection(o_hi, first_piece, base, norm_next, hbase):
                for n in range(2):
                    o_hi_parts(o_hi, n, base)
                for c in range(OUT_CHUNKS):
                    for j in range(PIECES):
                        if c == 0:
                            for n in O_TURNS.get(j, ()):
                                o_hi_parts(o_hi, n, base)
                        if c >= 1 and norm_next and j in (1, 2):
                            x_hi(sb["xb_hi"], sb["norm_b_sb"], 2 * (c - 1) + j - 1, PIECES)
                        if c >= 1 and j == 3:
                            act.wait_ge(h_ready, hbase + c)
                            act.wait_ge(ssq_done, sq_base(hbase) + TOK * (c - 1))
                            sum_squares(c - 1)
                        if first_piece + c * PIECES + j + RING < ALL_PIECES:
                            split(first_piece, c * PIECES + j + RING)

            def sq_base(hbase):
                return TOK * (OUT_CHUNKS + hbase)

            out_projection(sb["oa_hi"], OUT_A, 0, True, 0)
            for n in (6, 7):
                x_hi(sb["xb_hi"], sb["norm_b_sb"], n, PIECES)
            act.wait_ge(h_ready, OUT_CHUNKS)
            act.wait_ge(ssq_done, sq_base(0) + TOK * 3)
            sum_squares(3)

            tr0 = A_ITER * A_TR
            with act.Fori(0, B_ITER) as i:
                for c in range(B_CHUNKS):
                    for j in range(PIECES):
                        if 1 <= c <= V_B and j in (1, 2):
                            to = (q_t, k_t)[(c - 1) % 2]
                            copy_turned(to[:, 2 * (j - 1):2 * j, :], j - 1,
                                        i * B_TR + (tr0 + 2 * (c - 1) + j), 2 * SEQ)
                        if c == 7 and j in (1, 2):
                            act.wait_ge(max_ready, i + (A_ITER + 1))
                            for hd in range(2 * (j - 1), 2 * j):
                                for b, cut in ((0, slice(0, P)), (1, slice(P, SPAN))):
                                    last = act.activation(
                                        t_b[:, hd, :, cut], t_b[:, hd, :, cut], ACT.Exp,
                                        scale=SCALE, bias=nm[:, b, hd:hd + 1],
                                        accum_out=den[:, b, hd:hd + 1])
                                last.then_inc(exp_done, 1)
                        m = P_TURNS.get((c, j))
                        if m is not None:
                            for n in (m, m + 1):
                                copy_turned(pt_b[:, n, :], n % 2,
                                            i * B_TR + (tr0 + 4 * NG + n + 1), SPAN)
                        if j == PIECES - 1:
                            act.wait_ge(pe_used, i * PIECES_B + (LAYER_B + (c + 1) * PIECES))
                            if c == 0:
                                act.wait_ge(rstd_done, 2)
                            if c < V_B:
                                chunk_out(nat, c, rstd[:, 1])
                            elif c < Z_B:
                                chunk_out(sb["v_b"][:, c - V_B], c, rstd[:, 1])
                            else:
                                z_part(c, 1)
                        split(i * PIECES_B + LAYER_B, c * PIECES + j + RING)

            out_projection(sb["ob_hi"], OUT_B, PIECES, False, OUT_CHUNKS)
            act.wait_ge(h_ready, 2 * OUT_CHUNKS)
            act.wait_ge(ssq_done, sq_base(OUT_CHUNKS) + TOK * 3)
            sum_squares(3)
            act.wait_ge(rstd_done, 3)
            act.wait_ge(pre_done, OUT_CHUNKS)
            for n in range(2):
                cut = slice(D_MODEL // 2 * n, D_MODEL // 2 * (n + 1))
                act.activation(sb["final"][:, 0, cut], sb["final"][:, 0, cut], ACT.Copy,
                               scale=rstd[:, 2, 0:1]).then_inc(final_act, 1)

        @block.vector
        def _(dve):
            own = Links(dve, dve_link)
            link = own.link

            def split(n0, n):
                s = n % RING
                dve.wait_ge(hi_done, n0 + (n + 1))
                dve.tensor_tensor(w_lo[:, s], raw[:, s], w_hi[:, s], ALU.subtract
                                  ).then_inc(lo_done, 1)

            def x_lo(hi, lo, gain, n, base):
                dve.wait_ge(xt_hi, base + n + 1)
                for k in range(2):
                    kt = 2 * n + k
                    last = dve.scalar_tensor_tensor(
                        lo[:, kt, :], turned[:, n % 2, SEQ * k:SEQ * (k + 1)],
                        gain[:, kt:kt + 1], hi[:, kt, :], ALU.mult, ALU.subtract)
                last.then_inc(xt_lo, 1)

            def mean_square(count):
                dve.wait_ge(ssq_done, count)
                dve.tensor_reduce(ms[:, 0, 0:TOK], ssq[:, :, :], AX.X, ALU.add
                                  ).then_inc(ms_done, 1)

            def biased(to, n, slope, mask, count):
                dve.wait_ge(qk_done, count)
                dve.scalar_tensor_tensor(to, dist_sb[:, mask, :], slope, score[:, n % 2, 0:SPAN],
                                         ALU.mult, ALU.add).then_inc(t_ready, 1)

            def sigmoid(b, count):
                dve.wait_ge(z_exp, count)
                link(dve.tensor_scalar(e[:, b], e[:, b], 1.0, None, ALU.add))
                link(dve.reciprocal(e[:, b], e[:, b]))

            def gate(b, c, layer, o_nat, i):
                link(dve.scalar_tensor_tensor(e[:, b], proj[:, c % 2, b, :],
                                              rstd[:, layer, b:b + 1], e[:, b], ALU.mult,
                                              ALU.mult))
                return dve.tensor_tensor(o_nat[:, b, bass.ds(i * COLS, COLS)], e[:, b], og[:, b],
                                         ALU.mult)

            for n, value in enumerate((1.0 / D_MODEL, 1.0 / A_VDIM, RMS_EPS, -0.5)):
                dve.memset(consts[:, n, :], value).then_inc(dve_link, 1)
                own.n += 1
            for c in range(OUT_CHUNKS):
                for n in (2 * c, 2 * c + 1):
                    x_lo(sb["xa_hi"], sb["xa_lo"], sb["norm_a_sb"], n, 0)
                split(0, c)
            mean_square(TOK * OUT_CHUNKS)
            dve.wait_ge(rstd_done, 1)
            link(dve.tensor_scalar(nrstd[:, 0, :], rstd[:, 0, :], -1.0, None, ALU.mult))
            dve.wait_ge(const_landed, 7 * 16)
            lams_sb = sb["lams_sb"]
            for n in range(2):
                dve.tensor_tensor_reduce(sb["lam_prod"][:, n], lams_sb[:, 2 * n],
                                         lams_sb[:, 2 * n + 1], 1.0, 0.0, ALU.mult, ALU.add,
                                         lam[:, n:n + 1]).then_inc(lam_dot, 1)
            dve.tensor_scalar(sb["subln_sb"][:, :], sb["subln_sb"][:, :], 1.0 - LAM_INIT, None,
                              ALU.mult)
            dve.wait_ge(lam_exp, 1)
            link(dve.tensor_tensor(lam[:, 4:5], lam[:, 3:4], lam[:, 2:3], ALU.subtract))
            link(dve.tensor_scalar(lam[:, 5:6], lam[:, 4:5], -LAM_INIT, None, ALU.add))

            for j in range(PIECES):
                split(0, j + RING)
            before = own.n
            with dve.Fori(0, A_ITER) as i:
                own.base, own.n = i * A_STEPS + before, 0
                for c in range(1, A_CHUNKS + 1):
                    for j in range(PIECES):
                        if c == 2 and j in (4, 6):
                            hd = (j - 4) // 2
                            for n in (j - 4, j - 3):
                                biased(t_a[:, n, :], n, slopes_sb[:, bass.ds(2 * i + hd, 1)], 0,
                                       i * A_QK + (n + 1))
                        if c == 2 and j == 7:
                            dve.wait_ge(t_ready, i * A_QK + A_QK)
                            dve.tensor_reduce(rden[:, 0, :], t_a[:, :, 0:P], AX.X, ALU.max)
                            link(dve.tensor_reduce(rden[:, 1, :], t_a[:, :, P:SPAN], AX.X,
                                                   ALU.max))
                            dve.tensor_scalar(nm[:, :, :], rden[:, :, :], -SCALE, None, ALU.mult
                                              ).then_inc(max_ready, 1)
                        if c == 3 and j == 2:
                            dve.wait_ge(exp_done, i + 1)
                            link(dve.reciprocal(rden[:, :, :], den[:, :, :]))
                            for b, cut in ((0, slice(0, P)), (1, slice(P, SPAN))):
                                for hd in range(2):
                                    last = dve.tensor_scalar(
                                        p_a[:, hd, cut], t_a[:, 2 * hd + 1, cut],
                                        rden[:, b, 2 * hd + 1:2 * hd + 2], lam[:, 5:6], ALU.mult,
                                        ALU.mult)
                            link(last)
                            for b, cut in ((0, slice(0, P)), (1, slice(P, SPAN))):
                                for hd in range(2):
                                    last = dve.scalar_tensor_tensor(
                                        p_a[:, hd, cut], t_a[:, 2 * hd, cut],
                                        rden[:, b, 2 * hd:2 * hd + 1], p_a[:, hd, cut], ALU.mult,
                                        ALU.add)
                            last.then_inc(p_ready, 1)
                        if c == 3 and j == 5:
                            for hd in range(2):
                                dve.wait_ge(pv_done, i * A_PV + (hd + 1))
                                dve.tensor_copy(
                                    og[:, :, A_VDIM * hd:A_VDIM * (hd + 1)],
                                    score[:, hd, :].rearrange("p (b n) -> p b n", b=TOK)
                                ).then_inc(pv_out, 1)
                        if c == A_CHUNKS and j == 0:
                            dve.wait_ge(rstd2_done, i + 1)
                            for hd in range(2):
                                for b in range(TOK):
                                    part = og[:, b, A_VDIM * hd:A_VDIM * (hd + 1)]
                                    last = dve.scalar_tensor_tensor(
                                        part, part, rstd2[:, hd, b:b + 1], sb["subln_sb"][:, :],
                                        ALU.mult, ALU.mult)
                            link(last)
                        if c == A_CHUNKS and j in (1, 3):
                            sigmoid(j // 2, i * TOK + (j // 2 + 1))
                        if c == A_CHUNKS and j in (2, 4):
                            last = gate(j // 2 - 1, A_CHUNKS - 1, 0, sb["oa_nat"], i)
                            if j == 4:
                                last.then_inc(o_ready, 1)
                        split(i * PIECES_A, c * PIECES + j + RING)
                assert own.n == A_STEPS, own.n
            own.base, own.n = 0, before + A_ITER * A_STEPS

            def out_projection(first_piece, norm_next):
                for c in range(OUT_CHUNKS):
                    cut = slice(COLS * c, COLS * (c + 1))
                    for j in range(PIECES):
                        if c >= 1 and norm_next and j in (1, 2):
                            x_lo(sb["xb_hi"], sb["xb_lo"], sb["norm_b_sb"], 2 * (c - 1) + j - 1,
                                 PIECES)
                        if j == PIECES - 1:
                            dve.wait_ge(pe_used, first_piece + (c + 1) * PIECES)
                            dve.tensor_tensor(h[:, :, cut], h[:, :, cut], proj[:, c % 2, :, :],
                                              ALU.add).then_inc(h_ready, 1)
                        if c >= 1 and first_piece + c * PIECES + j + RING < ALL_PIECES:
                            split(first_piece, c * PIECES + j + RING)

            out_projection(OUT_A, True)
            for n in (6, 7):
                x_lo(sb["xb_hi"], sb["xb_lo"], sb["norm_b_sb"], n, PIECES)
            for j in range(PIECES):
                if j == 0:
                    mean_square(2 * TOK * OUT_CHUNKS)
                if j == 2:
                    dve.wait_ge(rstd_done, 2)
                    link(dve.tensor_scalar(nrstd[:, 1, :], rstd[:, 1, :], -1.0, None, ALU.mult))
                split(LAYER_B, j + RING)

            before = own.n
            qk0, pv0 = A_ITER * A_QK, A_ITER * A_PV
            with dve.Fori(0, B_ITER) as i:
                own.base, own.n = i * B_STEPS + before, 0
                for c in range(1, B_CHUNKS + 1):
                    for j in range(PIECES):
                        if c in (2, 4, 6) and j in (4, 6):
                            g = c // 2 - 1
                            for hd in (j - 4, j - 3):
                                biased(t_b[:, hd, g, :], hd,
                                       slopes_sb[:, bass.ds(B_HPI * i + (A_HEADS + hd), 1)],
                                       1 + g, i * B_QK + (qk0 + B_HPI * g + hd + 1))
                        if c == 6 and j == 7:
                            dve.wait_ge(t_ready, i * B_QK + (qk0 + B_QK))
                            link(dve.tensor_reduce(rden[:, 0, :], t_b[:, :, :, 0:P], AX.XY,
                                                   ALU.max))
                        if c == 7 and j == 0:
                            link(dve.tensor_reduce(rden[:, 1, :], t_b[:, :, :, P:SPAN], AX.XY,
                                                   ALU.max))
                            dve.tensor_scalar(nm[:, :, :], rden[:, :, :], -SCALE, None, ALU.mult
                                              ).then_inc(max_ready, 1)
                        if c == Z_B and j == 0:
                            dve.wait_ge(exp_done, i * B_HPI + (A_ITER + B_HPI))
                            link(dve.reciprocal(rden[:, :, :], den[:, :, :]))
                        if c == Z_B and 1 <= j <= B_HPI:
                            hd = j - 1
                            dve.wait_ge(pv_done, i * B_PV + (pv0 + hd + 1))
                            for b in range(TOK):
                                last = dve.tensor_scalar(
                                    og[:, b, HEAD * hd:HEAD * (hd + 1)],
                                    score[:, hd % 2, P * b:P * (b + 1)], rden[:, b, hd:hd + 1],
                                    None, ALU.mult)
                            last.then_inc(pv_out, 1)
                        if c == B_CHUNKS and j in (0, 2):
                            sigmoid(j // 2, i * TOK + (A_ITER * TOK + j // 2 + 1))
                        if c == B_CHUNKS and j in (1, 3):
                            if j == 1:
                                dve.wait_ge(pv_out, i * B_PV + (pv0 + B_PV))
                            last = gate(j // 2, Z_B, 1, sb["ob_nat"], i)
                            if j == 3:
                                last.then_inc(o_ready, 1)
                        split(i * PIECES_B + LAYER_B, c * PIECES + j + RING)
                assert own.n == B_STEPS, own.n
            own.base, own.n = 0, before + B_ITER * B_STEPS

            out_projection(OUT_B, False)
            mean_square(3 * TOK * OUT_CHUNKS)
            dve.wait_ge(rstd_done, 3)
            for n in range(2):
                cut = slice(D_MODEL // 2 * n, D_MODEL // 2 * (n + 1))
                dve.tensor_scalar(sb["final"][:, 1, cut], sb["final"][:, 1, cut],
                                  rstd[:, 2, 1:2], None, ALU.mult).then_inc(final_dve, 1)

        @block.gpsimd
        def _(pool):
            own = Links(pool, pool_link)

            def rsqrt(to, of, tmp, norm, done):
                wide = tmp.shape[1]
                own.link(pool.tensor_tensor(tmp, of, consts[:, norm, 0:wide], ALU.mult))
                own.link(pool.tensor_tensor(tmp, tmp, consts[:, 2, 0:wide], ALU.add))
                pool.tensor_tensor(to, tmp, consts[:, 3, 0:wide], ALU.pow).then_inc(done, 1)

            def token_norm(n):
                pool.wait_ge(ms_done, n + 1)
                rsqrt(rstd[:, n, :], ms[:, 0, 0:TOK], ms[:, 1, 0:TOK], 0, rstd_done)

            def o_lo_parts(o_hi, o_lo, base):
                for n in range(PIECES):
                    pool.wait_ge(ot_hi, base + n + 1)
                    pool.tensor_tensor(o_lo[:, 2 * n:2 * n + 2, :],
                                       nat[:, n % 2, :].rearrange("p (k s) -> p k s", k=2),
                                       o_hi[:, 2 * n:2 * n + 2, :], ALU.subtract
                                       ).then_inc(ot_lo, 1)

            pool.wait_ge(dve_link, 4)
            token_norm(0)
            before = own.n
            with pool.Fori(0, A_ITER) as i:
                own.base, own.n = i * 2 + before, 0
                pool.wait_ge(ssq2_done, i * 4 + 4)
                rsqrt(rstd2[:, :, :].rearrange("p a b -> p (a b)"),
                      ssq2[:, :, :].rearrange("p a b -> p (a b)"), ms[:, 1, 4:8], 1,
                      rstd2_done)
            own.base, own.n = 0, before + 2 * A_ITER
            o_lo_parts(sb["oa_hi"], sb["oa_lo"], 0)
            token_norm(1)
            o_lo_parts(sb["ob_hi"], sb["ob_lo"], PIECES)
            pool.wait_ge(normf_landed, 16)
            for c in range(OUT_CHUNKS):
                pool.wait_ge(h_ready, OUT_CHUNKS + c + 1)
                cut = slice(COLS * c, COLS * (c + 1))
                for b in range(TOK):
                    last = pool.tensor_tensor(sb["final"][:, b, cut], h[:, b, cut],
                                              sb["normf_sb"][:, cut], ALU.mult)
                last.then_inc(pre_done, 1)
            token_norm(2)


def distances():
    query = np.concatenate([np.repeat(np.arange(P)[:, None], P, 1),
                            np.repeat(P + np.arange(P)[:, None], SEQ, 1)], 1)
    key = np.concatenate([np.arange(P), np.arange(SEQ)])[None, :]
    far = query - key
    seen = [far >= 0]
    for window, dilation in B_GROUPS:
        seen.append((far >= 0) & (far % dilation == 0) & (far <= window))
    return np.stack([np.where(s, -far.astype(np.float32), np.float32(MASKED)) for s in seen],
                    1).astype(np.float32).reshape(P, -1)


def slope_table():
    slopes = [2.0 ** (-8.0 * (np.arange(n) + 1.0) / n) / SCALE for n in (A_HEADS, B_HEADS)]
    return np.tile(np.concatenate(slopes).astype(np.float32)[None, :], (P, 1))


def kernel(x, norm_a, w_in_a, lam_q1, lam_k1, lam_q2, lam_k2, subln_a, w_out_a, norm_b, w_in_b,
           w_out_b, norm_f):
    import concourse.bacc as bacc
    from concourse.bass_utils import run_bass_kernel_spmd

    def rows(v, n):
        return np.ascontiguousarray(np.broadcast_to(np.asarray(v).reshape(1, n), (P, n)))

    def by_tile(v):
        return np.ascontiguousarray(np.asarray(v).reshape(KT, P).T)

    arrays = {
        "x_dram": np.asarray(x)[0],
        "w_in_a_dram": np.asarray(w_in_a)[0],
        "w_out_a_dram": np.asarray(w_out_a)[0],
        "w_in_b_dram": np.asarray(w_in_b)[0],
        "w_out_b_dram": np.asarray(w_out_b)[0],
        "norm_a_dram": by_tile(norm_a),
        "norm_b_dram": by_tile(norm_b),
        "norm_f_dram": rows(norm_f, D_MODEL),
        "subln_dram": rows(subln_a, A_VDIM),
        "lams_dram": np.concatenate([rows(v, HEAD) for v in (lam_q1, lam_k1, lam_q2, lam_k2)], 1),
        "dist_dram": distances(),
        "slopes_dram": slope_table(),
        "ident_dram": np.eye(P, dtype=np.float32),
    }
    arrays = {k: np.ascontiguousarray(v) for k, v in arrays.items()}
    nc = bacc.Bacc("TRN2", target_bir_lowering=False, num_devices=1)
    ins = [nc.dram_tensor(k, v.shape, mybir.dt.from_np(v.dtype), kind="ExternalInput").ap()
           for k, v in arrays.items()]
    out = nc.dram_tensor("out_dram", (SEQ, D_MODEL), F32, kind="ExternalOutput").ap()
    hybrid(nc, *ins, out)
    got = run_bass_kernel_spmd(nc, [arrays], core_ids=[0])
    return got.results[0]["out_dram"].reshape(1, SEQ, D_MODEL)
```

```python
from contextlib import ExitStack
import math

import numpy as np

import concourse.bass as bass
from concourse import mybir
from concourse.alu_op_type import AluOpType as ALU

F32 = mybir.dt.float32
F32R = mybir.dt.float32r
ACT = mybir.ActivationFunctionType
AX = mybir.AxisListType

P = 128
D_MODEL = 2048
SEQ = 256
TOK = SEQ // P
KT = D_MODEL // P
COLS = 512
PIECE_KT = 2
PIECES = KT // PIECE_KT
RING = 4
OUT_CHUNKS = D_MODEL // COLS
HEAD = 128
SCALE = HEAD ** -0.5
RMS_EPS = 1e-6
A_HEADS = 8
A_VDIM = 256
A_ITER = 4
A_CHUNKS = 4
B_HEADS = 16
B_GROUPS = ((128, 1), (512, 4), (2048, 16))
NG = len(B_GROUPS)
B_ITER = 4
B_CHUNKS = 3 * NG + 1
B_HPI = B_HEADS // B_ITER
SPAN = P + SEQ
B_WIDTHS = tuple(SEQ if dilation % TOK else P for _, dilation in B_GROUPS)
B_STARTS = tuple(sum(B_WIDTHS[:g]) for g in range(NG))
B_SPAN = sum(B_WIDTHS)
DIST_STARTS = [SPAN + TOK * a for a in B_STARTS]
LAM_INIT = 0.8 - 0.6 * math.exp(0.0)
MASKED = -1.0e30

ROUNDS_A = A_CHUNKS * PIECES // RING
ROUNDS_B = B_CHUNKS * PIECES // RING
ROUNDS_OUT = OUT_CHUNKS * PIECES // RING
OUT_A = A_ITER * ROUNDS_A
LAYER_B = OUT_A + ROUNDS_OUT
OUT_B = LAYER_B + B_ITER * ROUNDS_B
ALL_PIECES = (OUT_B + ROUNDS_OUT) * RING
POOL_SLOT = RING - 1

A_TR, B_TR = 6, 4 * NG + TOK * B_HPI
A_NAT, B_NAT = 3, 3 * NG
A_QK, B_QK = 4, NG * B_HPI
A_PV, B_PV = 2, B_HPI
A_STEPS, B_STEPS = 10, 9

X_BANKS = 6

P_TURNS = {(7, 5): 0, (7, 6): 1, (7, 7): 2, (8, 1): 3}
FIRST_TURNS = 2
LATER_TURNS = PIECES - FIRST_TURNS
O_TURNS = {0: (2,), 1: (3,), 2: (4,), 3: (5,), 4: (6,), 6: (7,)}


class Links:

    def __init__(self, eng, sem):
        self.eng, self.sem, self.n, self.base = eng, sem, 0, 0

    def link(self, ins):
        self.n += 1
        ins.then_inc(self.sem, 1)
        self.eng.wait_ge(self.sem, self.base + self.n)


def hybrid(nc, x, w_in_a, w_out_a, w_in_b, w_out_b, norm_a, norm_b, norm_f, subln, lams, dist,
           slopes, ident, out):
    with ExitStack() as ctx:
        def sem(name):
            return ctx.enter_context(nc.semaphore(name))

        start = (nc.sbuf_base + 31) // 32 * 32
        total = [0]
        places = []

        def place(name, shape, dt, at=None):
            size = 4 * int(np.prod(shape[1:]))
            offset = total[0] if at is None else at
            if at is None:
                total[0] += (size + 31) // 32 * 32
            places.append((name, shape, dt, offset))
            return offset + size

        place("raw", [P, RING, PIECE_KT * COLS], F32)
        place("w_hi", [P, RING, PIECE_KT * COLS], F32R)
        place("w_lo", [P, RING, PIECE_KT * COLS], F32R)
        first = total[0]
        place("xa_hi", [P, KT, SEQ], F32R)
        place("xa_lo", [P, KT, SEQ], F32R)
        place("oa_hi", [P, KT, SEQ], F32R, first)
        place("oa_lo", [P, KT, SEQ], F32R, first + 4 * KT * SEQ)
        after = place("ob_nat", [P, TOK, D_MODEL], F32, first)
        place("v_b", [P, NG, TOK, COLS], F32, after)
        second = total[0]
        place("xb_hi", [P, KT, SEQ], F32R)
        place("xb_lo", [P, KT, SEQ], F32R)
        place("ob_hi", [P, KT, SEQ], F32R, second)
        place("ob_lo", [P, KT, SEQ], F32R, second + 4 * KT * SEQ)
        after = place("oa_nat", [P, TOK, D_MODEL], F32, second)
        after = place("v_a", [P, 1, TOK, COLS], F32, after)
        after = place("t_a", [P, 4, SPAN], F32, after)
        place("p_a", [P, 2, SPAN], F32, after)
        place("h", [P, TOK, D_MODEL], F32)
        place("nat", [P, TOK, COLS], F32)
        place("q_t", [P, 4, SEQ], F32)
        place("k_t", [P, 4, SEQ], F32)
        third = total[0]
        place("t_b", [P, B_HPI, TOK, B_SPAN], F32)
        place("pt_b", [P, B_HPI, TOK, B_SPAN], F32)
        place("pt_a", [P, 2, SPAN], F32, third)
        after = place("normf_sb", [P, D_MODEL], F32, third)
        place("final", [P, TOK, D_MODEL], F32, after)
        place("og", [P, TOK, COLS], F32)
        place("e", [P, TOK, COLS], F32)
        place("squares", [P, TOK, COLS], F32)
        place("dist_sb", [P, SPAN + TOK * B_SPAN], F32)
        place("ident_sb", [P, P], F32)
        place("slopes_sb", [P, A_HEADS + B_HEADS], F32)
        place("norm_a_sb", [P, KT], F32)
        place("norm_b_sb", [P, KT], F32)
        place("subln_sb", [P, A_VDIM], F32)
        place("lams_sb", [P, 4, HEAD], F32)
        place("lam_prod", [P, 2, HEAD], F32)
        place("lam", [P, 8], F32)
        place("nm", [P, 2, 4], F32)
        place("den", [P, 2, 4], F32)
        place("rden", [P, 2, 4], F32)
        place("ssq", [P, TOK, OUT_CHUNKS], F32)
        place("ssq2", [P, 2, TOK], F32)
        place("ms", [P, 2, 8], F32)
        place("rstd", [P, 3, TOK], F32)
        place("rstd_nat", [P, TOK], F32)
        place("nrstd", [P, 2, TOK], F32)
        place("rstd2", [P, 2, TOK], F32)
        place("consts", [P, 5, 8], F32)
        ctx.enter_context(nc.sbuf_tensor("arena", [P, total[0] // 4 + 8], F32))
        sb = {name: nc.alloc_sbuf_tensor_at(name, shape, dt, offset=start + offset)
              for name, shape, dt, offset in places}
        raw, w_hi, w_lo, h, nat = (sb[n] for n in ("raw", "w_hi", "w_lo", "h", "nat"))
        q_t, k_t, og, e = (sb[n] for n in ("q_t", "k_t", "og", "e"))
        squares, dist_sb, ident_sb, slopes_sb = (
            sb[n] for n in ("squares", "dist_sb", "ident_sb", "slopes_sb"))
        lam, nm, den, rden, ssq, ssq2, ms, rstd, rstd_nat, nrstd, rstd2, consts = (
            sb[n] for n in ("lam", "nm", "den", "rden", "ssq", "ssq2", "ms", "rstd",
                            "rstd_nat", "nrstd",
                            "rstd2", "consts"))
        t_a, p_a, pt_a, t_b, pt_b = (sb[n] for n in ("t_a", "p_a", "pt_a", "t_b", "pt_b"))

        proj = ctx.enter_context(nc.psum_tensor("proj", [P, 2, TOK, COLS], F32))
        turned = ctx.enter_context(nc.psum_tensor("turned", [P, 2, COLS], F32))
        score = ctx.enter_context(nc.psum_tensor("score", [P, 2, COLS], F32))

        landed = [sem(f"landed{s}") for s in range(RING)]
        x_landed = [sem(f"x_landed{c}") for c in range(OUT_CHUNKS)]
        first_landed = sem("first_landed")
        const_landed = sem("const_landed")
        normf_landed = sem("normf_landed")
        hi_done = sem("hi_done")
        lo_done = [sem(f"lo_done{s}") for s in range(RING)]
        pe_used = sem("pe_used")
        xt_turned = sem("xt_turned")
        xt_hi = sem("xt_hi")
        xt_lo = sem("xt_lo")
        ot_turned = sem("ot_turned")
        ot_hi = sem("ot_hi")
        first_lo = sem("first_lo")
        ot_lo = sem("ot_lo")
        tr_turned = sem("tr_turned")
        tr_copied = sem("tr_copied")
        nat_ready = sem("nat_ready")
        qk_done = sem("qk_done")
        t_ready = sem("t_ready")
        max_ready = sem("max_ready")
        exp_done = sem("exp_done")
        p_ready = sem("p_ready")
        pv_done = sem("pv_done")
        pv_out = sem("pv_out")
        ssq2_done = sem("ssq2_done")
        rstd2_done = sem("rstd2_done")
        z_exp = sem("z_exp")
        o_ready = sem("o_ready")
        h_ready = sem("h_ready")
        ssq_done = sem("ssq_done")
        ms_done = sem("ms_done")
        rstd_done = sem("rstd_done")
        rstd_moved = sem("rstd_moved")
        lam_dot = sem("lam_dot")
        lam_exp = sem("lam_exp")
        dve_link = sem("dve_link")
        pool_link = sem("pool_link")
        pre_done = sem("pre_done")
        last_pre = sem("last_pre")
        final_act = sem("final_act")
        final_dve = sem("final_dve")
        stored = sem("stored")

        w_a = w_in_a.rearrange("(t p) n -> p t n", p=P)
        w_b = w_in_b.rearrange("(t p) n -> p t n", p=P)
        wo_a = w_out_a.rearrange("(t p) n -> p t n", p=P)
        wo_b = w_out_b.rearrange("(t p) n -> p t n", p=P)
        x_v = x.rearrange("(b p) n -> p b n", p=P)
        out_v = out.rearrange("(b p) n -> p b n", p=P)

        b_first = [(3 * g + s) * D_MODEL for g in range(NG) for s in (0, 1)]
        b_first += [(3 * g + 2) * D_MODEL for g in range(NG)] + [3 * NG * D_MODEL]
        V_B, Z_B = 2 * NG, B_CHUNKS - 1

        def x_bank(n, base):
            free = [turned[:, 0], turned[:, 1], score[:, 0], score[:, 1], proj[:, 1, 0],
                    proj[:, 1, 1]]
            assert len(free) == X_BANKS
            return turned[:, n % 2] if base or n >= X_BANKS else free[n]

        def x_parts(to, n, k, base):
            to, of = to[:, 2 * n + k, :], x_bank(n, base)[:, SEQ * k:SEQ * (k + 1)]
            if base:
                to = to.rearrange("p (b q) -> p q b", b=TOK)
                of = of.rearrange("p (q b) -> p q b", b=TOK)
            return to, of

        def o_parts(to, n, layer):
            to, of = to[:, 2 * n:2 * n + 2, :], turned[:, n % 2, :]
            if layer:
                return (to.rearrange("p k (q b) -> p k b q", b=TOK),
                        of.rearrange("p (k b q) -> p k b q", k=2, b=TOK))
            return to, of.rearrange("p (k s) -> p k s", k=2)

        def lo_part(eng, r0, n):
            s = n % RING
            eng.wait_ge(hi_done, r0 * RING + (n + 1))
            eng.tensor_tensor(w_lo[:, s], raw[:, s], w_hi[:, s], ALU.subtract
                              ).then_inc(lo_done[s], 1)

        block = ctx.enter_context(nc.Block())

        @block.sync
        def _(sp):
            def piece(view, col, r0, c, j):
                s, n = j % RING, c * PIECES + j
                if not isinstance(r0, int) or r0 + n // RING > 0:
                    sp.wait_ge(lo_done[s], r0 + n // RING)
                sp.dma_start(raw[:, s].rearrange("p (t n) -> p t n", t=PIECE_KT),
                             view[:, PIECE_KT * j:PIECE_KT * (j + 1), col]
                             ).then_inc(landed[s], 16)

            def columns(start):
                return bass.ds(start, COLS)

            for c in range(OUT_CHUNKS):
                if c == OUT_CHUNKS - 1:
                    piece(w_a, slice(0, COLS), 0, 0, 0)
                sp.dma_start(h[:, :, COLS * c:COLS * (c + 1)],
                             x_v[:, :, COLS * c:COLS * (c + 1)]).then_inc(x_landed[c], 16)
            for j in range(1, RING):
                piece(w_a, slice(0, COLS), 0, 0, j)
            for to, of in ((sb["norm_b_sb"][:, :], norm_b), (slopes_sb[:, :], slopes),
                           (sb["subln_sb"][:, :], subln),
                           (sb["lams_sb"][:, :, :].rearrange("p a b -> p (a b)"), lams),
                           (dist_sb[:, :], dist)):
                sp.dma_start(to, of).then_inc(const_landed, 16)
            for c in range(A_CHUNKS):
                for j in range(PIECES):
                    if c * PIECES + j >= RING:
                        piece(w_a, slice(c * D_MODEL, c * D_MODEL + COLS), 0, c, j)
            with sp.Fori(1, A_ITER) as i:
                for c in range(A_CHUNKS):
                    for j in range(PIECES):
                        piece(w_a, columns(i * COLS + c * D_MODEL), i * ROUNDS_A, c, j)
            for c in range(OUT_CHUNKS):
                for j in range(PIECES):
                    piece(wo_a, slice(c * COLS, c * COLS + COLS), OUT_A, c, j)
            with sp.Fori(0, B_ITER) as i:
                for c in range(B_CHUNKS):
                    for j in range(PIECES):
                        piece(w_b, columns(i * COLS + b_first[c]), i * ROUNDS_B + LAYER_B, c, j)
            sp.wait_ge(tr_copied, A_ITER * A_TR + B_ITER * B_TR)
            sp.dma_start(sb["normf_sb"][:, :], norm_f).then_inc(normf_landed, 16)
            for c in range(OUT_CHUNKS):
                for j in range(PIECES):
                    piece(wo_b, slice(c * COLS, c * COLS + COLS), OUT_B, c, j)
            half_cols = D_MODEL // 2
            for n in range(2):
                cut = slice(half_cols * n, half_cols * (n + 1))
                sp.wait_ge(final_act, n + 1)
                sp.dma_start(out_v[:, 0, cut], sb["final"][:, 0, cut]).then_inc(stored, 16)
                sp.wait_ge(final_dve, n + 1)
                sp.dma_start(out_v[:, 1, cut], sb["final"][:, 1, cut]).then_inc(stored, 16)
            sp.wait_ge(stored, 4 * 16)

        @block.tensor
        def _(pe):
            def turn(bank, at, of):
                return pe.matmul(bank[:, at:at + P], of, ident_sb[:, :],
                                 start=True, stop=True, is_transpose=True)

            def split_ready(r0, c, j):
                pe.wait_ge(lo_done[j % RING], r0 + ((c * PIECES + j) // RING + 1))

            def matmuls(lhs_hi, lhs_lo, c, j):
                s = j % RING
                for k in range(PIECE_KT):
                    kt = PIECE_KT * j + k
                    cut = slice(COLS * k, COLS * (k + 1))
                    for b in range(TOK):
                        tok = slice(P * b, P * (b + 1))
                        to = proj[:, c % 2, b, :]
                        pe.matmul(to, lhs_hi[:, kt, tok], w_hi[:, s, cut], start=(kt == 0),
                                  stop=False)
                        pe.matmul(to, lhs_hi[:, kt, tok], w_lo[:, s, cut], start=False, stop=False)
                        last = pe.matmul(to, lhs_lo[:, kt, tok], w_hi[:, s, cut], start=False,
                                         stop=(kt == KT - 1))
                last.then_inc(pe_used, 1)

            def turn_x(c, half_c, n, base):
                for k in range(2):
                    for b in range(TOK):
                        col = COLS * c + P * (2 * half_c + k)
                        last = turn(x_bank(n, base), SEQ * k + P * b, h[:, b, col:col + P])
                last.then_inc(xt_turned, 1)

            def turn_nat(first_block, bank):
                for k in range(2):
                    for b in range(TOK):
                        col = P * (first_block + k)
                        last = turn(turned[:, bank], SEQ * k + P * b, nat[:, b, col:col + P])
                last.then_inc(tr_turned, 1)

            def product(to, q, k):
                return pe.matmul(to, q, k, start=True, stop=True)

            def scores_a(n, bank):
                product(score[:, bank, 0:P], q_t[:, n, 0:P], k_t[:, n, 0:P])
                product(score[:, bank, P:SPAN], q_t[:, n, P:SEQ], k_t[:, n, :]
                        ).then_inc(qk_done, 1)

            def scores_b(n, g, bank):
                for b in range(TOK):
                    own_keys = slice(P * b, P * (b + 1))
                    width = B_WIDTHS[g]
                    last = product(score[:, bank, width * b:width * (b + 1)], q_t[:, n, own_keys],
                                   k_t[:, n, slice(0, SEQ) if width == SEQ else own_keys])
                last.then_inc(qk_done, 1)

            def turn_p(of, bank):
                for n in range(of.shape[1] // P):
                    last = turn(turned[:, bank], P * n, of[:, P * n:P * (n + 1)])
                last.then_inc(tr_turned, 1)

            pe.wait_ge(first_landed, 32)
            for n in range(2 * OUT_CHUNKS):
                pe.wait_ge(x_landed[n // 2], 16)
                if n >= X_BANKS:
                    pe.wait_ge(xt_lo, n - X_BANKS + 1)
                turn_x(n // 2, n % 2, n, 0)

            def turn_o(n, o_nat, layer):
                pe.wait_ge(o_ready, layer * TOK * A_ITER + n + 1)
                if n in (2, 3):
                    pe.wait_ge(first_lo, layer * FIRST_TURNS + n - 1)
                elif n > 3:
                    pe.wait_ge(ot_hi, layer * PIECES + n - 1)
                for k in range(2):
                    for b in range(TOK):
                        last = turn(turned[:, n % 2], SEQ * k + P * b,
                                    o_nat[:, b, P * (2 * n + k):P * (2 * n + k + 1)])
                last.then_inc(ot_turned, 1)

            def iteration_a(i, last_one):
                for c in range(A_CHUNKS):
                    for j in range(PIECES):
                        if c in (1, 2) and j in (1, 2):
                            if j == 1:
                                pe.wait_ge(nat_ready, i * A_NAT + c)
                            if c == 2:
                                pe.wait_ge(tr_copied, i * A_TR + j)
                            turn_nat(2 * (j - 1), j - 1)
                        if c == 2 and j in (4, 6):
                            pe.wait_ge(tr_copied, i * A_TR + 4)
                            if j == 6:
                                pe.wait_ge(t_ready, i * A_QK + 2)
                            for n in range(2):
                                scores_a(j - 4 + n, n)
                        if c == 3 and j == 5:
                            pe.wait_ge(p_ready, i + 1)
                            for n in range(2):
                                turn_p(p_a[:, n], n)
                        if c == 3 and j == 6:
                            pe.wait_ge(tr_copied, i * A_TR + A_TR)
                            pe.wait_ge(nat_ready, i * A_NAT + A_NAT)
                            for n in range(2):
                                v = sb["v_a"][:, 0, :, A_VDIM * n:A_VDIM * (n + 1)]
                                pe.matmul(score[:, n, 0:A_VDIM], pt_a[:, n, 0:P], v[:, 0],
                                          start=True, stop=True)
                                pe.matmul(score[:, n, A_VDIM:], pt_a[:, n, P:2 * P], v[:, 0],
                                          start=True, stop=False)
                                pe.matmul(score[:, n, A_VDIM:], pt_a[:, n, 2 * P:], v[:, 1],
                                          start=False, stop=True).then_inc(pv_done, 1)
                        if last_one and (c, j) == (A_CHUNKS - 1, PIECES - 1):
                            for n in range(FIRST_TURNS):
                                turn_o(n, sb["oa_nat"], 0)
                        if c == 0:
                            pe.wait_ge(xt_lo, j + 1)
                        split_ready(i * ROUNDS_A, c, j)
                        matmuls(sb["xa_hi"], sb["xa_lo"], c, j)

            with pe.Fori(0, A_ITER - 1) as i:
                iteration_a(i, False)
            iteration_a(A_ITER - 1, True)

            def out_projection(o_nat, o_hi, o_lo, first_round, layer, turn_h):
                for c in range(OUT_CHUNKS):
                    for j in range(PIECES):
                        if c == 0:
                            for n in O_TURNS.get(j, ()):
                                turn_o(n, o_nat, layer)
                            if j < FIRST_TURNS:
                                pe.wait_ge(first_lo, layer * FIRST_TURNS + j + 1)
                            else:
                                pe.wait_ge(ot_lo, layer * LATER_TURNS + j - FIRST_TURNS + 1)
                        if c >= 1 and turn_h and j in (1, 2):
                            n = 2 * (c - 1) + j - 1
                            pe.wait_ge(h_ready, c)
                            if n >= 2:
                                pe.wait_ge(xt_lo, PIECES + n - 1)
                            turn_x(c - 1, j - 1, n, PIECES)
                        split_ready(first_round, c, j)
                        matmuls(o_hi, o_lo, c, j)

            out_projection(sb["oa_nat"], sb["oa_hi"], sb["oa_lo"], OUT_A, 0, True)
            pe.wait_ge(h_ready, OUT_CHUNKS)
            for n in (6, 7):
                pe.wait_ge(xt_lo, PIECES + n - 1)
                turn_x(3, n - 6, n, PIECES)

            tr0, nat0, qk0 = A_ITER * A_TR, A_ITER * A_NAT, A_ITER * A_QK
            pv0 = A_ITER * A_PV
            def iteration_b(i, last_one):
                for c in range(B_CHUNKS):
                    for j in range(PIECES):
                        if 1 <= c <= V_B and j in (1, 2):
                            if j == 1:
                                pe.wait_ge(nat_ready, i * B_NAT + (nat0 + c))
                            if c >= 2:
                                pe.wait_ge(tr_copied, i * B_TR + (tr0 + 2 * (c - 1) + j - 2))
                            turn_nat(2 * (j - 1), j - 1)
                        if c in (2, 4, 6) and j in (4, 6):
                            pe.wait_ge(tr_copied, i * B_TR + (tr0 + 2 * c))
                            n0 = 4 * (c // 2 - 1) + (j - 4)
                            if n0 >= 2:
                                pe.wait_ge(t_ready, i * B_QK + (qk0 + n0))
                            for n in range(2):
                                scores_b(j - 4 + n, c // 2 - 1, n)
                        hd = P_TURNS.get((c, j))
                        if hd is not None:
                            pe.wait_ge(exp_done, i * B_HPI + (A_ITER + hd + 1))
                            for b in range(TOK):
                                pe.wait_ge(tr_copied,
                                           i * B_TR + (tr0 + 4 * NG + TOK * hd + b - 1))
                                turn_p(t_b[:, hd, b], b)
                        if c == Z_B and 1 <= j <= B_HPI:
                            hd = j - 1
                            pe.wait_ge(tr_copied,
                                       i * B_TR + (tr0 + 4 * NG + TOK * (hd + 1)))
                            pe.wait_ge(nat_ready, i * B_NAT + (nat0 + B_NAT))
                            if hd >= 2:
                                pe.wait_ge(pv_out, i * B_PV + (pv0 + hd - 1))
                            v = sb["v_b"][:, :, :, HEAD * hd:HEAD * (hd + 1)]
                            for b in range(TOK):
                                keys = [(g, k) for g in range(NG) for k in range(TOK)
                                        if B_WIDTHS[g] == SEQ or k == b]
                                for n, (g, k) in enumerate(keys):
                                    last = pe.matmul(
                                        score[:, hd % 2, P * b:P * (b + 1)],
                                        sb["pt_b"][:, hd, b, P * n:P * (n + 1)], v[:, g, k],
                                        start=(n == 0), stop=(n == len(keys) - 1))
                            last.then_inc(pv_done, 1)
                        if last_one and (c, j) == (Z_B, PIECES - 1):
                            for n in range(FIRST_TURNS):
                                turn_o(n, sb["ob_nat"], 1)
                        if c == 0:
                            pe.wait_ge(xt_lo, PIECES + j + 1)
                        split_ready(i * ROUNDS_B + LAYER_B, c, j)
                        matmuls(sb["xb_hi"], sb["xb_lo"], c, j)

            with pe.Fori(0, B_ITER - 1) as i:
                iteration_b(i, False)
            iteration_b(B_ITER - 1, True)

            out_projection(sb["ob_nat"], sb["ob_hi"], sb["ob_lo"], OUT_B, 1, False)

        @block.scalar
        def _(act):
            def split(r0, n):
                s, r = n % RING, n // RING
                act.wait_ge(landed[s], r0 * 16 + 16 * (r + 1))
                if not isinstance(r0, int) or r0 + r > 0:
                    act.wait_ge(pe_used, r0 * RING + (n - RING + 1))
                act.activation(w_hi[:, s], raw[:, s], ACT.Copy).then_inc(hi_done, 1)

            def chunk_out(to, c, scale_by):
                for b in range(TOK):
                    last = act.activation(to[:, b], proj[:, c % 2, b, :], ACT.Copy,
                                          scale=scale_by[:, b:b + 1])
                last.then_inc(nat_ready, 1)

            def copy_turned(to, bank, n, width):
                act.wait_ge(tr_turned, n)
                act.activation(to, turned[:, bank, 0:width], ACT.Copy).then_inc(tr_copied, 1)

            def x_hi(x_hi_sb, gain, n, base):
                act.wait_ge(xt_turned, base + n + 1)
                for k in range(2):
                    to, of = x_parts(x_hi_sb, n, k, base)
                    last = act.activation(to, of, ACT.Copy, scale=gain[:, 2 * n + k:2 * n + k + 1])
                last.then_inc(xt_hi, 1)

            def sum_squares(c):
                for b in range(TOK):
                    last = act.activation(squares[:, b], h[:, b, COLS * c:COLS * (c + 1)],
                                          ACT.Square, accum_out=ssq[:, b, c:c + 1])
                    last.then_inc(ssq_done, 1)

            def z_part(c, layer):
                for b in range(TOK):
                    act.activation(e[:, b], proj[:, c % 2, b, :], ACT.Exp,
                                   scale=nrstd[:, layer, b:b + 1]).then_inc(z_exp, 1)

            act.dma_start(ident_sb[:, :], ident).then_inc(first_landed, 16)
            act.dma_start(sb["norm_a_sb"][:, :], norm_a).then_inc(first_landed, 16)
            act.wait_ge(dve_link, 4)
            act.activation(consts[:, 4, :], consts[:, 2, :], ACT.Exp)
            act.wait_ge(first_landed, 32)
            for n in range(2 * OUT_CHUNKS):
                if n == X_BANKS:
                    split(0, 0)
                x_hi(sb["xa_hi"], sb["norm_a_sb"], n, 0)
            for n in range(1, RING):
                split(0, n)
            for c in range(OUT_CHUNKS):
                if c:
                    act.wait_ge(ssq_done, TOK * c)
                sum_squares(c)
            act.wait_ge(lam_dot, 2)
            act.activation(lam[:, 2:4], lam[:, 0:2], ACT.Exp).then_inc(lam_exp, 1)

            def o_hi_part(n, o_hi, layer):
                act.wait_ge(ot_turned, layer * PIECES + n + 1)
                copy, (hi, of) = nat[:, n % 2, :], o_parts(o_hi, n, layer)
                if n >= FIRST_TURNS:
                    if n >= FIRST_TURNS + 2:
                        act.wait_ge(ot_lo, layer * LATER_TURNS + n - FIRST_TURNS - 1)
                    if layer:
                        copy = copy.rearrange("p (k q b) -> p k b q", k=2, b=TOK)
                    act.activation(copy, of if layer else turned[:, n % 2, :], ACT.Copy)
                act.activation(hi, of, ACT.Copy).then_inc(ot_hi, 1)

            def iteration_a(i, last_one):
                for c in range(A_CHUNKS):
                    for j in range(PIECES):
                        if c in (1, 2) and j in (1, 2):
                            to = (q_t, k_t)[c - 1]
                            copy_turned(to[:, 2 * (j - 1):2 * j, :], j - 1,
                                        i * A_TR + (2 * (c - 1) + j), 2 * SEQ)
                        if c == 3 and j == 0:
                            act.wait_ge(max_ready, i + 1)
                            for n in range(4):
                                for b, cut in ((0, slice(0, P)), (1, slice(P, SPAN))):
                                    last = act.activation(
                                        t_a[:, n, cut], t_a[:, n, cut], ACT.Exp, scale=SCALE,
                                        bias=nm[:, b, n:n + 1], accum_out=den[:, b, n:n + 1])
                            last.then_inc(exp_done, 1)
                        if c == 3 and j == 5:
                            for n in range(2):
                                copy_turned(pt_a[:, n, :], n, i * A_TR + 5 + n, SPAN)
                        if c == 3 and j == 7:
                            act.wait_ge(pv_out, i * A_PV + A_PV)
                            for n in range(2):
                                for b in range(TOK):
                                    last = act.activation(
                                        squares[:, b, A_VDIM * n:A_VDIM * (n + 1)],
                                        og[:, b, A_VDIM * n:A_VDIM * (n + 1)], ACT.Square,
                                        accum_out=ssq2[:, n, b:b + 1])
                                    last.then_inc(ssq2_done, 1)
                        if last_one and (c, j) == (A_CHUNKS - 1, PIECES - 1):
                            for n in range(FIRST_TURNS):
                                o_hi_part(n, sb["oa_hi"], 0)
                        if j == PIECES - 1:
                            act.wait_ge(pe_used, i * (ROUNDS_A * RING) + (c + 1) * PIECES)
                            if c == 0:
                                act.wait_ge(rstd_done, 1)
                            if c < 2:
                                chunk_out(nat, c, rstd[:, 0])
                            elif c == 2:
                                chunk_out(sb["v_a"][:, 0], c, rstd[:, 0])
                            else:
                                z_part(c, 0)
                        split(i * ROUNDS_A, c * PIECES + j + RING)

            with act.Fori(0, A_ITER - 1) as i:
                iteration_a(i, False)
            iteration_a(A_ITER - 1, True)

            def out_projection(o_hi, first_round, layer, norm_next, hbase):
                for c in range(OUT_CHUNKS):
                    for j in range(PIECES):
                        if c == 0:
                            for n in O_TURNS.get(j, ()):
                                o_hi_part(n, o_hi, layer)
                        if c >= 1 and norm_next and j in (1, 2):
                            x_hi(sb["xb_hi"], sb["norm_b_sb"], 2 * (c - 1) + j - 1, PIECES)
                        if c >= 1 and j == 3:
                            act.wait_ge(h_ready, hbase + c)
                            act.wait_ge(ssq_done, sq_base(hbase) + TOK * (c - 1))
                            sum_squares(c - 1)
                        if first_round * RING + c * PIECES + j + RING < ALL_PIECES:
                            split(first_round, c * PIECES + j + RING)

            def sq_base(hbase):
                return TOK * (OUT_CHUNKS + hbase)

            out_projection(sb["oa_hi"], OUT_A, 0, True, 0)
            for n in (6, 7):
                x_hi(sb["xb_hi"], sb["norm_b_sb"], n, PIECES)
            act.wait_ge(h_ready, OUT_CHUNKS)
            act.wait_ge(ssq_done, sq_base(0) + TOK * 3)
            sum_squares(3)

            tr0 = A_ITER * A_TR
            def iteration_b(i, last_one):
                for c in range(B_CHUNKS):
                    for j in range(PIECES):
                        if 1 <= c <= V_B and j in (1, 2):
                            to = (q_t, k_t)[(c - 1) % 2]
                            copy_turned(to[:, 2 * (j - 1):2 * j, :], j - 1,
                                        i * B_TR + (tr0 + 2 * (c - 1) + j), 2 * SEQ)
                        if c == 7 and 1 <= j <= B_HPI:
                            hd = j - 1
                            act.wait_ge(max_ready, i + (A_ITER + 1))
                            for b in range(TOK):
                                last = act.activation(
                                    t_b[:, hd, b], t_b[:, hd, b], ACT.Exp, scale=SCALE,
                                    bias=nm[:, b, hd:hd + 1], accum_out=den[:, b, hd:hd + 1])
                            last.then_inc(exp_done, 1)
                        hd = P_TURNS.get((c, j))
                        if hd is not None:
                            for b in range(TOK):
                                copy_turned(pt_b[:, hd, b], b,
                                            i * B_TR + (tr0 + 4 * NG + TOK * hd + b + 1), B_SPAN)
                        if last_one and (c, j) == (Z_B, PIECES - 1):
                            for n in range(FIRST_TURNS):
                                o_hi_part(n, sb["ob_hi"], 1)
                        if j == PIECES - 1:
                            act.wait_ge(pe_used,
                                        i * (ROUNDS_B * RING) + (LAYER_B * RING + (c + 1) * PIECES))
                            if c == 0:
                                act.wait_ge(rstd_moved, 4 * 16)
                            if c < V_B:
                                chunk_out(nat, c, rstd[:, 1])
                            elif c < Z_B:
                                chunk_out(sb["v_b"][:, c - V_B], c, rstd[:, 1])
                            else:
                                z_part(c, 1)
                        split(i * ROUNDS_B + LAYER_B, c * PIECES + j + RING)

            with act.Fori(0, B_ITER - 1) as i:
                iteration_b(i, False)
            iteration_b(B_ITER - 1, True)

            out_projection(sb["ob_hi"], OUT_B, 1, False, OUT_CHUNKS)
            act.wait_ge(h_ready, 2 * OUT_CHUNKS)
            act.wait_ge(ssq_done, sq_base(OUT_CHUNKS) + TOK * 3)
            sum_squares(3)
            act.wait_ge(rstd_done, 3)
            act.wait_ge(pre_done, OUT_CHUNKS - 1)
            act.wait_ge(last_pre, TOK)
            for n in range(2):
                cut = slice(D_MODEL // 2 * n, D_MODEL // 2 * (n + 1))
                act.activation(sb["final"][:, 0, cut], sb["final"][:, 0, cut], ACT.Copy,
                               scale=rstd[:, 2, 0:1]).then_inc(final_act, 1)

        @block.vector
        def _(dve):
            own = Links(dve, dve_link)
            link = own.link

            def split(r0, n):
                if n % RING != POOL_SLOT:
                    lo_part(dve, r0, n)

            def x_lo(hi, lo, gain, n, base):
                dve.wait_ge(xt_hi, base + n + 1)
                for k in range(2):
                    to, of = x_parts(lo, n, k, base)
                    last = dve.scalar_tensor_tensor(to, of, gain[:, 2 * n + k:2 * n + k + 1],
                                                    x_parts(hi, n, k, base)[0], ALU.mult,
                                                    ALU.subtract)
                last.then_inc(xt_lo, 1)

            def o_lo_part(n, o_hi, o_lo, layer):
                dve.wait_ge(ot_hi, layer * PIECES + n + 1)
                lo, of = o_parts(o_lo, n, layer)
                dve.tensor_tensor(lo, of, o_parts(o_hi, n, layer)[0], ALU.subtract
                                  ).then_inc(first_lo, 1)

            def mean_square(count):
                dve.wait_ge(ssq_done, count)
                dve.tensor_reduce(ms[:, 0, 0:TOK], ssq[:, :, :], AX.X, ALU.add
                                  ).then_inc(ms_done, 1)

            def biased(to, n, slope, start, count):
                dve.wait_ge(qk_done, count)
                shape = to.shape
                minus_dist = dist_sb[:, start:start + shape[1] * shape[2]]
                of = score[:, n % 2, 0:shape[1] * shape[2]]
                minus_dist, of = (v.rearrange("p (b n) -> p b n", b=shape[1])
                                  for v in (minus_dist, of))
                dve.scalar_tensor_tensor(to, minus_dist, slope, of, ALU.mult, ALU.add
                                         ).then_inc(t_ready, 1)

            halves = [slice(0, COLS // 2), slice(COLS // 2, COLS)]

            def sigmoid(half, count):
                part = e[:, :, halves[half]]
                dve.wait_ge(z_exp, count)
                link(dve.tensor_scalar(part, part, 1.0, None, ALU.add))
                link(dve.reciprocal(part, part))

            def gate(half, c, layer, o_nat, i):
                cut = halves[half]
                for b in range(TOK):
                    last = dve.scalar_tensor_tensor(e[:, b, cut], proj[:, c % 2, b, cut],
                                                    rstd[:, layer, b:b + 1], e[:, b, cut],
                                                    ALU.mult, ALU.mult)
                link(last)
                dve.tensor_tensor(o_nat[:, :, bass.ds(i * COLS + cut.start, COLS // 2)],
                                  e[:, :, cut], og[:, :, cut], ALU.mult).then_inc(o_ready, 1)

            for n, value in enumerate((1.0 / D_MODEL, 1.0 / A_VDIM, RMS_EPS, -0.5)):
                dve.memset(consts[:, n, :], value).then_inc(dve_link, 1)
                own.n += 1
            for n in range(2 * OUT_CHUNKS):
                if n == X_BANKS:
                    split(0, 0)
                x_lo(sb["xa_hi"], sb["xa_lo"], sb["norm_a_sb"], n, 0)
            for n in range(1, RING):
                split(0, n)
            dve.wait_ge(const_landed, 5 * 16)
            lams_sb = sb["lams_sb"]
            for n in range(2):
                dve.tensor_tensor_reduce(sb["lam_prod"][:, n], lams_sb[:, 2 * n],
                                         lams_sb[:, 2 * n + 1], 1.0, 0.0, ALU.mult, ALU.add,
                                         lam[:, n:n + 1]).then_inc(lam_dot, 1)
            dve.tensor_scalar(sb["subln_sb"][:, :], sb["subln_sb"][:, :], 1.0 - LAM_INIT, None,
                              ALU.mult)

            for j in range(PIECES):
                if j == 1:
                    dve.wait_ge(lam_exp, 1)
                    link(dve.tensor_tensor(lam[:, 4:5], lam[:, 3:4], lam[:, 2:3], ALU.subtract))
                    link(dve.tensor_scalar(lam[:, 5:6], lam[:, 4:5], -LAM_INIT, None, ALU.add))
                    mean_square(TOK * OUT_CHUNKS)
                if j == 3:
                    dve.wait_ge(rstd_done, 1)
                    link(dve.tensor_scalar(nrstd[:, 0, :], rstd[:, 0, :], -1.0, None, ALU.mult))
                split(0, j + RING)
            before = own.n
            def iteration_a(i, last_one):
                own.base, own.n = i * A_STEPS + before, 0
                for c in range(1, A_CHUNKS + 1):
                    for j in range(PIECES):
                        if c == 2 and j in (4, 6):
                            hd = (j - 4) // 2
                            for n in (j - 4, j - 3):
                                biased(t_a[:, n:n + 1, :], n, slopes_sb[:, bass.ds(2 * i + hd, 1)], 0,
                                       i * A_QK + (n + 1))
                        if c == 2 and j == 7:
                            dve.wait_ge(t_ready, i * A_QK + A_QK)
                            dve.tensor_reduce(rden[:, 0, :], t_a[:, :, 0:P], AX.X, ALU.max)
                            link(dve.tensor_reduce(rden[:, 1, :], t_a[:, :, P:SPAN], AX.X,
                                                   ALU.max))
                            dve.tensor_scalar(nm[:, :, :], rden[:, :, :], -SCALE, None, ALU.mult
                                              ).then_inc(max_ready, 1)
                        if c == 3 and j == 2:
                            dve.wait_ge(exp_done, i + 1)
                            link(dve.reciprocal(rden[:, :, :], den[:, :, :]))
                            for b, cut in ((0, slice(0, P)), (1, slice(P, SPAN))):
                                for hd in range(2):
                                    last = dve.tensor_scalar(
                                        p_a[:, hd, cut], t_a[:, 2 * hd + 1, cut],
                                        rden[:, b, 2 * hd + 1:2 * hd + 2], lam[:, 5:6], ALU.mult,
                                        ALU.mult)
                            link(last)
                            for b, cut in ((0, slice(0, P)), (1, slice(P, SPAN))):
                                for hd in range(2):
                                    last = dve.scalar_tensor_tensor(
                                        p_a[:, hd, cut], t_a[:, 2 * hd, cut],
                                        rden[:, b, 2 * hd:2 * hd + 1], p_a[:, hd, cut], ALU.mult,
                                        ALU.add)
                            last.then_inc(p_ready, 1)
                        if c == 3 and j == 6:
                            for hd in range(2):
                                dve.wait_ge(pv_done, i * A_PV + (hd + 1))
                                dve.tensor_copy(
                                    og[:, :, A_VDIM * hd:A_VDIM * (hd + 1)],
                                    score[:, hd, :].rearrange("p (b n) -> p b n", b=TOK)
                                ).then_inc(pv_out, 1)
                        if last_one and (c, j) == (A_CHUNKS - 1, PIECES - 1):
                            for n in range(FIRST_TURNS):
                                o_lo_part(n, sb["oa_hi"], sb["oa_lo"], 0)
                        if c == A_CHUNKS and j == 0:
                            dve.wait_ge(rstd2_done, i + 1)
                            for hd in range(2):
                                for b in range(TOK):
                                    part = og[:, b, A_VDIM * hd:A_VDIM * (hd + 1)]
                                    last = dve.scalar_tensor_tensor(
                                        part, part, rstd2[:, hd, b:b + 1], sb["subln_sb"][:, :],
                                        ALU.mult, ALU.mult)
                            link(last)
                        if c == A_CHUNKS and j in (1, 3):
                            sigmoid(j // 2, i * TOK + TOK)
                        if c == A_CHUNKS and j in (2, 4):
                            gate(j // 2 - 1, A_CHUNKS - 1, 0, sb["oa_nat"], i)
                        split(i * ROUNDS_A, c * PIECES + j + RING)
                assert own.n == A_STEPS, own.n

            with dve.Fori(0, A_ITER - 1) as i:
                iteration_a(i, False)
            iteration_a(A_ITER - 1, True)
            own.base, own.n = 0, before + A_ITER * A_STEPS

            def out_projection(first_round, norm_next):
                for c in range(OUT_CHUNKS):
                    cut = slice(COLS * c, COLS * (c + 1))
                    for j in range(PIECES):
                        if c >= 1 and norm_next and j in (1, 2):
                            x_lo(sb["xb_hi"], sb["xb_lo"], sb["norm_b_sb"], 2 * (c - 1) + j - 1,
                                 PIECES)
                        if j == PIECES - 1:
                            dve.wait_ge(pe_used, first_round * RING + (c + 1) * PIECES)
                            dve.tensor_tensor(h[:, :, cut], h[:, :, cut], proj[:, c % 2, :, :],
                                              ALU.add).then_inc(h_ready, 1)
                        if c >= 1 and first_round * RING + c * PIECES + j + RING < ALL_PIECES:
                            split(first_round, c * PIECES + j + RING)

            out_projection(OUT_A, True)
            for n in (6, 7):
                x_lo(sb["xb_hi"], sb["xb_lo"], sb["norm_b_sb"], n, PIECES)
            for j in range(PIECES):
                if j == 0:
                    mean_square(2 * TOK * OUT_CHUNKS)
                if j == 4:
                    dve.wait_ge(rstd_moved, 4 * 16)
                    link(dve.tensor_scalar(nrstd[:, 1, :], rstd[:, 1, :], -1.0, None, ALU.mult))
                split(LAYER_B, j + RING)

            before = own.n
            qk0, pv0 = A_ITER * A_QK, A_ITER * A_PV
            def iteration_b(i, last_one):
                own.base, own.n = i * B_STEPS + before, 0
                for c in range(1, B_CHUNKS + 1):
                    for j in range(PIECES):
                        if c in (2, 4, 6) and j in (4, 6):
                            g = c // 2 - 1
                            for hd in (j - 4, j - 3):
                                biased(t_b[:, hd, :, B_STARTS[g]:B_STARTS[g] + B_WIDTHS[g]], hd,
                                       slopes_sb[:, bass.ds(B_HPI * i + (A_HEADS + hd), 1)],
                                       DIST_STARTS[g], i * B_QK + (qk0 + B_HPI * g + hd + 1))
                        if (c, j) in ((6, 7), (7, 0)):
                            two = slice(2 * (c - 6), 2 * (c - 6) + 2)
                            dve.wait_ge(t_ready, i * B_QK + (qk0 + B_QK))
                            link(dve.tensor_reduce(rden[:, :, two].rearrange("p b h -> p h b"),
                                                   t_b[:, two], AX.X, ALU.max))
                        if c == 7 and j == 0:
                            dve.tensor_scalar(nm[:, :, :], rden[:, :, :], -SCALE, None, ALU.mult
                                              ).then_inc(max_ready, 1)
                        if c == Z_B and j == 0:
                            dve.wait_ge(exp_done, i * B_HPI + (A_ITER + B_HPI))
                            link(dve.reciprocal(rden[:, :, :], den[:, :, :]))
                        if c == Z_B and 1 <= j <= B_HPI:
                            hd = j - 1
                            dve.wait_ge(pv_done, i * B_PV + (pv0 + hd + 1))
                            for b in range(TOK):
                                last = dve.tensor_scalar(
                                    og[:, b, HEAD * hd:HEAD * (hd + 1)],
                                    score[:, hd % 2, P * b:P * (b + 1)], rden[:, b, hd:hd + 1],
                                    None, ALU.mult)
                            last.then_inc(pv_out, 1)
                        if last_one and (c, j) == (Z_B, PIECES - 1):
                            for n in range(FIRST_TURNS):
                                o_lo_part(n, sb["ob_hi"], sb["ob_lo"], 1)
                        if c == B_CHUNKS and j in (0, 2):
                            sigmoid(j // 2, i * TOK + (A_ITER * TOK + TOK))
                        if c == B_CHUNKS and j in (1, 3):
                            if j == 1:
                                dve.wait_ge(pv_out, i * B_PV + (pv0 + B_PV))
                            gate(j // 2, Z_B, 1, sb["ob_nat"], i)
                        split(i * ROUNDS_B + LAYER_B, c * PIECES + j + RING)
                assert own.n == B_STEPS, own.n

            with dve.Fori(0, B_ITER - 1) as i:
                iteration_b(i, False)
            iteration_b(B_ITER - 1, True)
            own.base, own.n = 0, before + B_ITER * B_STEPS

            out_projection(OUT_B, False)
            dve.wait_ge(h_ready, 2 * OUT_CHUNKS)
            cut = slice(D_MODEL - COLS, D_MODEL)
            for b in range(TOK):
                dve.tensor_tensor(sb["final"][:, b, cut], h[:, b, cut], sb["normf_sb"][:, cut],
                                  ALU.mult).then_inc(last_pre, 1)
            mean_square(3 * TOK * OUT_CHUNKS)
            dve.wait_ge(rstd_done, 3)
            dve.wait_ge(last_pre, TOK)
            dve.wait_ge(pre_done, OUT_CHUNKS - 1)
            for n in range(2):
                cut = slice(D_MODEL // 2 * n, D_MODEL // 2 * (n + 1))
                dve.tensor_scalar(sb["final"][:, 1, cut], sb["final"][:, 1, cut],
                                  rstd[:, 2, 1:2], None, ALU.mult).then_inc(final_dve, 1)

        @block.gpsimd
        def _(pool):
            own = Links(pool, pool_link)

            def rsqrt(to, of, tmp, norm, done):
                wide = tmp.shape[1]
                own.link(pool.tensor_tensor(tmp, of, consts[:, norm, 0:wide], ALU.mult))
                own.link(pool.tensor_tensor(tmp, tmp, consts[:, 2, 0:wide], ALU.add))
                pool.tensor_tensor(to, tmp, consts[:, 3, 0:wide], ALU.pow).then_inc(done, 1)

            def token_norm(n):
                pool.wait_ge(ms_done, n + 1)
                rsqrt(rstd_nat[:, :] if n == 1 else rstd[:, n, :], ms[:, 0, 0:TOK], ms[:, 1, 0:TOK], 0, rstd_done)

            def split(r0, n):
                if n % RING == POOL_SLOT and r0 * RING + n < ALL_PIECES:
                    lo_part(pool, r0, n)

            def o_lo_part(o_hi, o_lo, n, layer):
                pool.wait_ge(ot_hi, layer * PIECES + n + 1)
                pool.tensor_tensor(o_lo[:, 2 * n:2 * n + 2, :],
                                   nat[:, n % 2, :].rearrange("p (k s) -> p k s", k=2),
                                   o_hi[:, 2 * n:2 * n + 2, :], ALU.subtract).then_inc(ot_lo, 1)

            def out_projection(o_hi, o_lo, first_round, layer):
                for c in range(OUT_CHUNKS):
                    for j in range(PIECES):
                        if c == 0:
                            for n in O_TURNS.get(j, ()):
                                o_lo_part(o_hi, o_lo, n, layer)
                        if c >= 1 and j == 1 and layer == 1:
                            pool.wait_ge(h_ready, OUT_CHUNKS + c)
                            cut = slice(COLS * (c - 1), COLS * c)
                            for b in range(TOK):
                                last = pool.tensor_tensor(sb["final"][:, b, cut], h[:, b, cut],
                                                          sb["normf_sb"][:, cut], ALU.mult)
                            last.then_inc(pre_done, 1)
                        split(first_round, c * PIECES + j + RING)

            pool.wait_ge(dve_link, 4)
            split(0, POOL_SLOT)
            token_norm(0)
            before = own.n
            with pool.Fori(0, A_ITER) as i:
                own.base, own.n = i * 2 + before, 0
                for r in range(1, ROUNDS_A + 1):
                    if r == ROUNDS_A:
                        pool.wait_ge(ssq2_done, i * 4 + 4)
                        rsqrt(rstd2[:, :, :].rearrange("p a b -> p (a b)"),
                              ssq2[:, :, :].rearrange("p a b -> p (a b)"), ms[:, 1, 4:8], 1,
                              rstd2_done)
                    lo_part(pool, i * ROUNDS_A, r * RING + POOL_SLOT)
            own.base, own.n = 0, before + 2 * A_ITER
            out_projection(sb["oa_hi"], sb["oa_lo"], OUT_A, 0)
            token_norm(1)
            pool.wait_ge(rstd_done, 2)
            for b in range(TOK):
                for k in range(TOK):
                    rows = slice(P // 2 * k, P // 2 * (k + 1))
                    pool.dma_start(rstd[rows, 1, b:b + 1], rstd_nat[b:P:TOK, k:k + 1]
                                   ).then_inc(rstd_moved, 16)
            with pool.Fori(0, B_ITER) as i:
                for r in range(1, ROUNDS_B + 1):
                    lo_part(pool, i * ROUNDS_B + LAYER_B, r * RING + POOL_SLOT)
            pool.wait_ge(normf_landed, 16)
            out_projection(sb["ob_hi"], sb["ob_lo"], OUT_B, 1)
            token_norm(2)


def distances():
    def part(query, key, dilation, window):
        far = query[:, None] - key[None, :]
        seen = (far >= 0) & (far % dilation == 0) & (far <= window)
        return np.where(seen, -far.astype(np.float32), np.float32(MASKED))

    place = np.arange(P)
    parts = [part(place, place, 1, SEQ), part(P + place, np.arange(SEQ), 1, SEQ)]
    tokens = [TOK * place + b for b in range(TOK)]
    for (window, dilation), width in zip(B_GROUPS, B_WIDTHS):
        for b in range(TOK):
            keys = np.concatenate(tokens) if width == SEQ else tokens[b]
            parts.append(part(tokens[b], keys, dilation, window))
    return np.concatenate(parts, 1).astype(np.float32)


def slope_table():
    slopes = [2.0 ** (-8.0 * (np.arange(n) + 1.0) / n) / SCALE for n in (A_HEADS, B_HEADS)]
    return np.tile(np.concatenate(slopes).astype(np.float32)[None, :], (P, 1))


def kernel(x, norm_a, w_in_a, lam_q1, lam_k1, lam_q2, lam_k2, subln_a, w_out_a, norm_b, w_in_b,
           w_out_b, norm_f):
    import concourse.bacc as bacc
    from concourse.bass_utils import run_bass_kernel_spmd

    def rows(v, n):
        return np.ascontiguousarray(np.broadcast_to(np.asarray(v).reshape(1, n), (P, n)))

    def by_tile(v):
        return np.ascontiguousarray(np.asarray(v).reshape(KT, P).T)

    arrays = {
        "x_dram": np.asarray(x)[0],
        "w_in_a_dram": np.asarray(w_in_a)[0],
        "w_out_a_dram": np.asarray(w_out_a)[0],
        "w_in_b_dram": np.asarray(w_in_b)[0],
        "w_out_b_dram": np.asarray(w_out_b)[0],
        "norm_a_dram": by_tile(norm_a),
        "norm_b_dram": by_tile(norm_b),
        "norm_f_dram": rows(norm_f, D_MODEL),
        "subln_dram": rows(subln_a, A_VDIM),
        "lams_dram": np.concatenate([rows(v, HEAD) for v in (lam_q1, lam_k1, lam_q2, lam_k2)], 1),
        "dist_dram": distances(),
        "slopes_dram": slope_table(),
        "ident_dram": np.eye(P, dtype=np.float32),
    }
    arrays = {k: np.ascontiguousarray(v) for k, v in arrays.items()}
    nc = bacc.Bacc("TRN2", target_bir_lowering=False, num_devices=1)
    ins = [nc.dram_tensor(k, v.shape, mybir.dt.from_np(v.dtype), kind="ExternalInput").ap()
           for k, v in arrays.items()]
    out = nc.dram_tensor("out_dram", (SEQ, D_MODEL), F32, kind="ExternalOutput").ap()
    hybrid(nc, *ins, out)
    got = run_bass_kernel_spmd(nc, [arrays], core_ids=[0])
    return got.results[0]["out_dram"].reshape(1, SEQ, D_MODEL)
```

```python
from contextlib import ExitStack
import math

import numpy as np

import concourse.bass as bass
from concourse import mybir
from concourse.alu_op_type import AluOpType as ALU

F32 = mybir.dt.float32
F32R = mybir.dt.float32r
ACT = mybir.ActivationFunctionType
AX = mybir.AxisListType

P = 128
D_MODEL = 2048
SEQ = 256
TOK = SEQ // P
KT = D_MODEL // P
COLS = 512
PIECE_KT = 2
PIECES = KT // PIECE_KT
RING = 4
OUT_CHUNKS = D_MODEL // COLS
HEAD = 128
SCALE = HEAD ** -0.5
RMS_EPS = 1e-6
A_HEADS = 8
A_VDIM = 256
A_ITER = 4
A_CHUNKS = 4
B_HEADS = 16
B_GROUPS = ((128, 1), (512, 4), (2048, 16))
NG = len(B_GROUPS)
B_ITER = 4
B_CHUNKS = 3 * NG + 1
B_HPI = B_HEADS // B_ITER
SPAN = P + SEQ
B_WIDTHS = tuple(SEQ if dilation % TOK else P for _, dilation in B_GROUPS)
B_STARTS = tuple(sum(B_WIDTHS[:g]) for g in range(NG))
B_SPAN = sum(B_WIDTHS)
DIST_STARTS = [SPAN + TOK * a for a in B_STARTS]
LAM_INIT = 0.8 - 0.6 * math.exp(0.0)
MASKED = -1.0e30

HALVES = (slice(0, COLS // 2), slice(COLS // 2, COLS))
LAST_PARTS = ((0, slice(0, COLS)), (1, HALVES[0]), (1, HALVES[1]))
SQ_COLS = OUT_CHUNKS + 1
SQ_NORM = TOK * SQ_COLS

ROUNDS_A = A_CHUNKS * PIECES // RING
ROUNDS_B = B_CHUNKS * PIECES // RING
ROUNDS_OUT = OUT_CHUNKS * PIECES // RING
OUT_A = A_ITER * ROUNDS_A
LAYER_B = OUT_A + ROUNDS_OUT
OUT_B = LAYER_B + B_ITER * ROUNDS_B
ALL_PIECES = (OUT_B + ROUNDS_OUT) * RING
POOL_SLOT = RING - 1

A_TR, B_TR = 6, 4 * NG + TOK * B_HPI
A_NAT, B_NAT = 3, 3 * NG
A_QK, B_QK = 4, NG * B_HPI
A_PV, B_PV = 2, B_HPI
A_STEPS, B_STEPS = 10, 9

X_BANKS = 6
PIECE_BEFORE_X = {4: 0, 5: 1, 6: 2}

P_TURNS = {(7, 5): 0, (7, 6): 1, (7, 7): 2, (8, 1): 3}
FIRST_TURNS, FIRST_TURNS_SLOT = 2, 6
O_TURNS = {0: (2,), 1: (3,), 2: (4,), 3: (5,), 4: (6,), 6: (7,)}
DIRECT_LO = (0, 1, 7)
COPIED_LO = (2, 3, 4, 5, 6)

STORES = ((1, 0), (0, 0), (1, 1), (1, 2), (0, 1), (1, 3), (0, 2), (0, 3))
DVE_STORES = ((1, 0), (1, 1), (1, 2), (1, 3), (0, 3))


class Links:

    def __init__(self, eng, sem):
        self.eng, self.sem, self.n, self.base = eng, sem, 0, 0

    def link(self, ins):
        self.n += 1
        ins.then_inc(self.sem, 1)
        self.eng.wait_ge(self.sem, self.base + self.n)


def hybrid(nc, x, w_in_a, w_out_a, w_in_b, w_out_b, first_in, norm_b, norm_f, subln, lams,
           dist, slopes, out):
    with ExitStack() as ctx:
        def sem(name):
            return ctx.enter_context(nc.semaphore(name))

        start = (nc.sbuf_base + 31) // 32 * 32
        total = [0]
        places = []

        def place(name, shape, dt, at=None):
            size = 4 * int(np.prod(shape[1:]))
            offset = total[0] if at is None else at
            if at is None:
                total[0] += (size + 31) // 32 * 32
            places.append((name, shape, dt, offset))
            return offset + size

        place("raw", [P, RING, PIECE_KT * COLS], F32)
        place("w_hi", [P, RING, PIECE_KT * COLS], F32R)
        place("w_lo", [P, RING, PIECE_KT * COLS], F32R)
        first = total[0]
        place("xa_hi", [P, KT, SEQ], F32R)
        place("xa_lo", [P, KT, SEQ], F32R)
        place("oa_hi", [P, KT, SEQ], F32R, first)
        place("oa_lo", [P, KT, SEQ], F32R, first + 4 * KT * SEQ)
        after = place("ob_nat", [P, TOK, D_MODEL], F32, first)
        place("v_b", [P, NG, TOK, COLS], F32, after)
        second = total[0]
        place("xb_hi", [P, KT, SEQ], F32R)
        place("xb_lo", [P, KT, SEQ], F32R)
        place("ob_hi", [P, KT, SEQ], F32R, second)
        place("ob_lo", [P, KT, SEQ], F32R, second + 4 * KT * SEQ)
        after = place("oa_nat", [P, TOK, D_MODEL], F32, second)
        after = place("v_a", [P, 1, TOK, COLS], F32, after)
        after = place("t_a", [P, 4, SPAN], F32, after)
        place("p_a", [P, 2, SPAN], F32, after)
        place("h", [P, TOK, D_MODEL], F32)
        place("nat", [P, TOK, COLS], F32)
        place("q_t", [P, 4, SEQ], F32)
        place("k_t", [P, 4, SEQ], F32)
        third = total[0]
        place("t_b", [P, B_HPI, TOK, B_SPAN], F32)
        place("pt_b", [P, B_HPI, TOK, B_SPAN], F32)
        place("pt_a", [P, 2, SPAN], F32, third)
        after = place("normf_sb", [P, D_MODEL], F32, third)
        place("final", [P, TOK, D_MODEL], F32, after)
        place("og", [P, TOK, COLS], F32)
        place("e", [P, TOK, COLS], F32)
        place("squares", [P, TOK, COLS], F32)
        place("dist_sb", [P, SPAN + TOK * B_SPAN], F32)
        place("first_sb", [P, P + KT], F32)
        place("slopes_sb", [P, A_HEADS + B_HEADS], F32)
        place("norm_b_sb", [P, KT], F32)
        place("subln_sb", [P, A_VDIM], F32)
        place("lams_sb", [P, 4, HEAD], F32)
        place("lam_prod", [P, 2, HEAD], F32)
        place("lam", [P, 8], F32)
        place("nm", [P, 2, 4], F32)
        place("den", [P, 2, 4], F32)
        place("rden", [P, 2, 4], F32)
        place("ssq", [P, TOK, SQ_COLS], F32)
        place("ssq2", [P, 2, TOK], F32)
        place("ms", [P, 2, 8], F32)
        place("rstd", [P, 3, TOK], F32)
        place("rstd_nat", [P, TOK], F32)
        place("nrstd", [P, 2, TOK], F32)
        place("rstd2", [P, 2, TOK], F32)
        place("consts", [P, 5, 8], F32)
        ctx.enter_context(nc.sbuf_tensor("arena", [P, total[0] // 4 + 8], F32))
        sb = {name: nc.alloc_sbuf_tensor_at(name, shape, dt, offset=start + offset)
              for name, shape, dt, offset in places}
        raw, w_hi, w_lo, h, nat = (sb[n] for n in ("raw", "w_hi", "w_lo", "h", "nat"))
        q_t, k_t, og, e = (sb[n] for n in ("q_t", "k_t", "og", "e"))
        squares, dist_sb, slopes_sb = (sb[n] for n in ("squares", "dist_sb", "slopes_sb"))
        ident_sb, norm_a_sb = sb["first_sb"][:, 0:P], sb["first_sb"][:, P:]
        lam, nm, den, rden, ssq, ssq2, ms, rstd, rstd_nat, nrstd, rstd2, consts = (
            sb[n] for n in ("lam", "nm", "den", "rden", "ssq", "ssq2", "ms", "rstd",
                            "rstd_nat", "nrstd",
                            "rstd2", "consts"))
        t_a, p_a, pt_a, t_b, pt_b = (sb[n] for n in ("t_a", "p_a", "pt_a", "t_b", "pt_b"))

        proj = ctx.enter_context(nc.psum_tensor("proj", [P, 2, TOK, COLS], F32))
        turned = ctx.enter_context(nc.psum_tensor("turned", [P, 2, COLS], F32))
        score = ctx.enter_context(nc.psum_tensor("score", [P, 2, COLS], F32))

        landed = [sem(f"landed{s}") for s in range(RING)]
        x_landed = [sem(f"x_landed{c}") for c in range(OUT_CHUNKS)]
        first_landed = sem("first_landed")
        const_landed = sem("const_landed")
        normf_landed = sem("normf_landed")
        hi_done = sem("hi_done")
        lo_done = [sem(f"lo_done{s}") for s in range(RING)]
        pe_used = sem("pe_used")
        xt_turned = sem("xt_turned")
        xt_hi = sem("xt_hi")
        xt_lo = sem("xt_lo")
        ot_turned = sem("ot_turned")
        ot_hi = sem("ot_hi")
        direct_lo = sem("direct_lo")
        copied_lo = sem("copied_lo")
        tr_turned = sem("tr_turned")
        tr_copied = sem("tr_copied")
        nat_ready = sem("nat_ready")
        qk_done = sem("qk_done")
        t_ready = sem("t_ready")
        max_ready = sem("max_ready")
        exp_done = sem("exp_done")
        p_ready = sem("p_ready")
        pv_done = sem("pv_done")
        pv_out = sem("pv_out")
        ssq2_done = sem("ssq2_done")
        rstd2_done = sem("rstd2_done")
        z_exp = sem("z_exp")
        o_ready = sem("o_ready")
        tile_done = sem("tile_done")
        h_ready = sem("h_ready")
        last_h = sem("last_h")
        ssq_done = sem("ssq_done")
        ms_done = sem("ms_done")
        rstd_done = sem("rstd_done")
        rstd_moved = sem("rstd_moved")
        lam_dot = sem("lam_dot")
        lam_exp = sem("lam_exp")
        dve_link = sem("dve_link")
        pool_link = sem("pool_link")
        pre_done = sem("pre_done")
        last_pre = sem("last_pre")
        final_act = sem("final_act")
        final_dve = sem("final_dve")
        stored = sem("stored")

        w_a = w_in_a.rearrange("(t p) n -> p t n", p=P)
        w_b = w_in_b.rearrange("(t p) n -> p t n", p=P)
        wo_a = w_out_a.rearrange("(t p) n -> p t n", p=P)
        wo_b = w_out_b.rearrange("(t p) n -> p t n", p=P)
        x_v = x.rearrange("(b p) n -> p b n", p=P)
        out_v = out.rearrange("(b p) n -> p b n", p=P)

        b_first = [(3 * g + s) * D_MODEL for g in range(NG) for s in (0, 1)]
        b_first += [(3 * g + 2) * D_MODEL for g in range(NG)] + [3 * NG * D_MODEL]
        V_B, Z_B = 2 * NG, B_CHUNKS - 1

        def x_bank(n, base):
            free = [turned[:, 0], turned[:, 1], score[:, 0], score[:, 1], proj[:, 1, 0],
                    proj[:, 1, 1]]
            assert len(free) == X_BANKS
            return turned[:, n % 2] if base or n >= X_BANKS else free[n]

        def x_parts(to, n, k, base):
            to, of = to[:, 2 * n + k, :], x_bank(n, base)[:, SEQ * k:SEQ * (k + 1)]
            if base:
                to = to.rearrange("p (b q) -> p q b", b=TOK)
                of = of.rearrange("p (q b) -> p q b", b=TOK)
            return to, of

        def o_parts(to, n, layer):
            to, of = to[:, 2 * n:2 * n + 2, :], turned[:, n % 2, :]
            if layer:
                return (to.rearrange("p k (q b) -> p k b q", b=TOK),
                        of.rearrange("p (k b q) -> p k b q", k=2, b=TOK))
            return to, of.rearrange("p (k s) -> p k s", k=2)

        def lo_part(eng, r0, n):
            s = n % RING
            eng.wait_ge(hi_done, r0 * RING + (n + 1))
            eng.tensor_tensor(w_lo[:, s], raw[:, s], w_hi[:, s], ALU.subtract
                              ).then_inc(lo_done[s], 1)

        block = ctx.enter_context(nc.Block())

        @block.sync
        def _(sp):
            def piece(view, col, r0, c, j):
                s, n = j % RING, c * PIECES + j
                if not isinstance(r0, int) or r0 + n // RING > 0:
                    sp.wait_ge(lo_done[s], r0 + n // RING)
                sp.dma_start(raw[:, s].rearrange("p (t n) -> p t n", t=PIECE_KT),
                             view[:, PIECE_KT * j:PIECE_KT * (j + 1), col]
                             ).then_inc(landed[s], 16)

            def columns(start):
                return bass.ds(start, COLS)

            for c in range(OUT_CHUNKS):
                if c == 2:
                    piece(w_a, slice(0, COLS), 0, 0, 0)
                sp.dma_start(h[:, :, COLS * c:COLS * (c + 1)],
                             x_v[:, :, COLS * c:COLS * (c + 1)]).then_inc(x_landed[c], 16)
            for j in range(1, RING):
                piece(w_a, slice(0, COLS), 0, 0, j)
            for to, of in ((sb["norm_b_sb"][:, :], norm_b), (slopes_sb[:, :], slopes),
                           (sb["subln_sb"][:, :], subln),
                           (sb["lams_sb"][:, :, :].rearrange("p a b -> p (a b)"), lams),
                           (dist_sb[:, :], dist)):
                sp.dma_start(to, of).then_inc(const_landed, 16)
            for c in range(A_CHUNKS):
                for j in range(PIECES):
                    if c * PIECES + j >= RING:
                        piece(w_a, slice(c * D_MODEL, c * D_MODEL + COLS), 0, c, j)
            with sp.Fori(1, A_ITER) as i:
                for c in range(A_CHUNKS):
                    for j in range(PIECES):
                        piece(w_a, columns(i * COLS + c * D_MODEL), i * ROUNDS_A, c, j)
            for c in range(OUT_CHUNKS):
                for j in range(PIECES):
                    piece(wo_a, slice(c * COLS, c * COLS + COLS), OUT_A, c, j)
            with sp.Fori(0, B_ITER) as i:
                for c in range(B_CHUNKS):
                    for j in range(PIECES):
                        piece(w_b, columns(i * COLS + b_first[c]), i * ROUNDS_B + LAYER_B, c, j)
            sp.wait_ge(tr_copied, A_ITER * A_TR + B_ITER * B_TR)
            sp.dma_start(sb["normf_sb"][:, :], norm_f).then_inc(normf_landed, 16)
            for c in range(OUT_CHUNKS):
                for j in range(PIECES):
                    piece(wo_b, slice(c * COLS, c * COLS + COLS), OUT_B, c, j)
            for b, c in STORES:
                cut = slice(COLS * c, COLS * (c + 1))
                if (b, c) in DVE_STORES:
                    sp.wait_ge(final_dve, DVE_STORES.index((b, c)) + 1)
                else:
                    sp.wait_ge(final_act, c + 1)
                sp.dma_start(out_v[:, b, cut], sb["final"][:, b, cut]).then_inc(stored, 16)
            sp.wait_ge(stored, len(STORES) * 16)

        @block.tensor
        def _(pe):
            def turn(bank, at, of):
                return pe.matmul(bank[:, at:at + P], of, ident_sb[:, :],
                                 start=True, stop=True, is_transpose=True)

            def split_ready(r0, c, j):
                pe.wait_ge(lo_done[j % RING], r0 + ((c * PIECES + j) // RING + 1))

            def product3(lhs_hi, lhs_lo, c, j, k, b):
                s, kt = j % RING, PIECE_KT * j + k
                cut, tok = slice(COLS * k, COLS * (k + 1)), slice(P * b, P * (b + 1))
                to = proj[:, c % 2, b, :]
                pe.matmul(to, lhs_hi[:, kt, tok], w_hi[:, s, cut], start=(kt == 0), stop=False)
                pe.matmul(to, lhs_hi[:, kt, tok], w_lo[:, s, cut], start=False, stop=False)
                return pe.matmul(to, lhs_lo[:, kt, tok], w_hi[:, s, cut], start=False,
                                 stop=(kt == KT - 1))

            def matmuls(lhs_hi, lhs_lo, c, j):
                for k in range(PIECE_KT):
                    for b in range(TOK):
                        last = product3(lhs_hi, lhs_lo, c, j, k, b)
                last.then_inc(pe_used, 1)

            def last_matmuls(lhs_hi, lhs_lo):
                for b, done in ((0, tile_done), (1, pe_used)):
                    for k in range(PIECE_KT):
                        last = product3(lhs_hi, lhs_lo, OUT_CHUNKS - 1, PIECES - 1, k, b)
                    last.then_inc(done, 1)

            def turn_x(n, base, tiles=(0, 1), complete=True):
                for b in tiles:
                    for k in range(2):
                        col = P * (2 * n + k)
                        last = turn(x_bank(n, base), SEQ * k + P * b, h[:, b, col:col + P])
                if complete:
                    last.then_inc(xt_turned, 1)

            def turn_nat(first_block, bank):
                for k in range(2):
                    for b in range(TOK):
                        col = P * (first_block + k)
                        last = turn(turned[:, bank], SEQ * k + P * b, nat[:, b, col:col + P])
                last.then_inc(tr_turned, 1)

            def product(to, q, k):
                return pe.matmul(to, q, k, start=True, stop=True)

            def scores_a(n, bank):
                product(score[:, bank, 0:P], q_t[:, n, 0:P], k_t[:, n, 0:P])
                product(score[:, bank, P:SPAN], q_t[:, n, P:SEQ], k_t[:, n, :]
                        ).then_inc(qk_done, 1)

            def scores_b(n, g, bank):
                for b in range(TOK):
                    own_keys = slice(P * b, P * (b + 1))
                    width = B_WIDTHS[g]
                    last = product(score[:, bank, width * b:width * (b + 1)], q_t[:, n, own_keys],
                                   k_t[:, n, slice(0, SEQ) if width == SEQ else own_keys])
                last.then_inc(qk_done, 1)

            def turn_p(of, bank):
                for n in range(of.shape[1] // P):
                    last = turn(turned[:, bank], P * n, of[:, P * n:P * (n + 1)])
                last.then_inc(tr_turned, 1)

            pe.wait_ge(first_landed, 16)
            for n in range(2 * OUT_CHUNKS):
                pe.wait_ge(x_landed[n // 2], 16)
                if n >= X_BANKS:
                    pe.wait_ge(xt_lo, n - X_BANKS + 1)
                turn_x(n, 0)

            def wait_lo(n, layer):
                if n in DIRECT_LO:
                    pe.wait_ge(direct_lo, layer * len(DIRECT_LO) + DIRECT_LO.index(n) + 1)
                else:
                    pe.wait_ge(copied_lo, layer * len(COPIED_LO) + COPIED_LO.index(n) + 1)

            def turn_o(n, o_nat, layer):
                pe.wait_ge(o_ready, layer * TOK * A_ITER + n + 1)
                if n >= 2:
                    if n - 2 in DIRECT_LO:
                        wait_lo(n - 2, layer)
                    else:
                        pe.wait_ge(ot_hi, layer * PIECES + n - 1)
                for k in range(2):
                    for b in range(TOK):
                        last = turn(turned[:, n % 2], SEQ * k + P * b,
                                    o_nat[:, b, P * (2 * n + k):P * (2 * n + k + 1)])
                last.then_inc(ot_turned, 1)

            def iteration_a(i, last_one):
                for c in range(A_CHUNKS):
                    for j in range(PIECES):
                        if c in (1, 2) and j in (1, 2):
                            if j == 1:
                                pe.wait_ge(nat_ready, i * A_NAT + c)
                            if c == 2:
                                pe.wait_ge(tr_copied, i * A_TR + j)
                            turn_nat(2 * (j - 1), j - 1)
                        if c == 2 and j in (4, 6):
                            pe.wait_ge(tr_copied, i * A_TR + 4)
                            if j == 6:
                                pe.wait_ge(t_ready, i * A_QK + 2)
                            for n in range(2):
                                scores_a(j - 4 + n, n)
                        if c == 3 and j == 5:
                            pe.wait_ge(p_ready, i + 1)
                            for n in range(2):
                                turn_p(p_a[:, n], n)
                        if c == 3 and j == 6:
                            pe.wait_ge(tr_copied, i * A_TR + A_TR)
                            pe.wait_ge(nat_ready, i * A_NAT + A_NAT)
                            for n in range(2):
                                v = sb["v_a"][:, 0, :, A_VDIM * n:A_VDIM * (n + 1)]
                                pe.matmul(score[:, n, 0:A_VDIM], pt_a[:, n, 0:P], v[:, 0],
                                          start=True, stop=True)
                                pe.matmul(score[:, n, A_VDIM:], pt_a[:, n, P:2 * P], v[:, 0],
                                          start=True, stop=False)
                                pe.matmul(score[:, n, A_VDIM:], pt_a[:, n, 2 * P:], v[:, 1],
                                          start=False, stop=True).then_inc(pv_done, 1)
                        if last_one and (c, j) == (A_CHUNKS - 1, FIRST_TURNS_SLOT):
                            for n in range(FIRST_TURNS):
                                turn_o(n, sb["oa_nat"], 0)
                        if c == 0:
                            pe.wait_ge(xt_lo, j + 1)
                        split_ready(i * ROUNDS_A, c, j)
                        matmuls(sb["xa_hi"], sb["xa_lo"], c, j)

            with pe.Fori(0, A_ITER - 1) as i:
                iteration_a(i, False)
            iteration_a(A_ITER - 1, True)

            def out_projection(o_nat, o_hi, o_lo, first_round, layer, turn_h):
                for c in range(OUT_CHUNKS):
                    for j in range(PIECES):
                        if c == 0:
                            for n in O_TURNS.get(j, ()):
                                turn_o(n, o_nat, layer)
                            wait_lo(j, layer)
                        if c >= 1 and turn_h and j in (1, 2):
                            n = 2 * (c - 1) + j - 1
                            pe.wait_ge(h_ready, c)
                            if n >= 2:
                                pe.wait_ge(xt_lo, PIECES + n - 1)
                            turn_x(n, PIECES)
                        split_ready(first_round, c, j)
                        if (c, j) == (OUT_CHUNKS - 1, PIECES - 1):
                            last_matmuls(o_hi, o_lo)
                        else:
                            matmuls(o_hi, o_lo, c, j)

            out_projection(sb["oa_nat"], sb["oa_hi"], sb["oa_lo"], OUT_A, 0, True)
            for b in range(TOK):
                for n in (6, 7):
                    pe.wait_ge(last_h, 1 if b == 0 else n - 4)
                    if b == 0:
                        pe.wait_ge(xt_lo, PIECES + n - 1)
                    turn_x(n, PIECES, (b,), b == TOK - 1)

            tr0, nat0, qk0 = A_ITER * A_TR, A_ITER * A_NAT, A_ITER * A_QK
            pv0 = A_ITER * A_PV

            def iteration_b(i, last_one):
                for c in range(B_CHUNKS):
                    for j in range(PIECES):
                        if 1 <= c <= V_B and j in (1, 2):
                            if j == 1:
                                pe.wait_ge(nat_ready, i * B_NAT + (nat0 + c))
                            if c >= 2:
                                pe.wait_ge(tr_copied, i * B_TR + (tr0 + 2 * (c - 1) + j - 2))
                            turn_nat(2 * (j - 1), j - 1)
                        if c in (2, 4, 6) and j in (4, 6):
                            pe.wait_ge(tr_copied, i * B_TR + (tr0 + 2 * c))
                            n0 = 4 * (c // 2 - 1) + (j - 4)
                            if n0 >= 2:
                                pe.wait_ge(t_ready, i * B_QK + (qk0 + n0))
                            for n in range(2):
                                scores_b(j - 4 + n, c // 2 - 1, n)
                        hd = P_TURNS.get((c, j))
                        if hd is not None:
                            pe.wait_ge(exp_done, i * B_HPI + (A_ITER + hd + 1))
                            for b in range(TOK):
                                pe.wait_ge(tr_copied,
                                           i * B_TR + (tr0 + 4 * NG + TOK * hd + b - 1))
                                turn_p(t_b[:, hd, b], b)
                        if c == Z_B and 1 <= j <= B_HPI:
                            hd = j - 1
                            pe.wait_ge(tr_copied,
                                       i * B_TR + (tr0 + 4 * NG + TOK * (hd + 1)))
                            pe.wait_ge(nat_ready, i * B_NAT + (nat0 + B_NAT))
                            if hd >= 2:
                                pe.wait_ge(pv_out, i * B_PV + (pv0 + hd - 1))
                            v = sb["v_b"][:, :, :, HEAD * hd:HEAD * (hd + 1)]
                            for b in range(TOK):
                                keys = [(g, k) for g in range(NG) for k in range(TOK)
                                        if B_WIDTHS[g] == SEQ or k == b]
                                for n, (g, k) in enumerate(keys):
                                    last = pe.matmul(
                                        score[:, hd % 2, P * b:P * (b + 1)],
                                        sb["pt_b"][:, hd, b, P * n:P * (n + 1)], v[:, g, k],
                                        start=(n == 0), stop=(n == len(keys) - 1))
                            last.then_inc(pv_done, 1)
                        if last_one and (c, j) == (Z_B, FIRST_TURNS_SLOT):
                            for n in range(FIRST_TURNS):
                                turn_o(n, sb["ob_nat"], 1)
                        if c == 0:
                            pe.wait_ge(xt_lo, PIECES + j + 1)
                        split_ready(i * ROUNDS_B + LAYER_B, c, j)
                        matmuls(sb["xb_hi"], sb["xb_lo"], c, j)

            with pe.Fori(0, B_ITER - 1) as i:
                iteration_b(i, False)
            iteration_b(B_ITER - 1, True)

            out_projection(sb["ob_nat"], sb["ob_hi"], sb["ob_lo"], OUT_B, 1, False)

        @block.scalar
        def _(act):
            def split(r0, n):
                s, r = n % RING, n // RING
                act.wait_ge(landed[s], r0 * 16 + 16 * (r + 1))
                if not isinstance(r0, int) or r0 + r > 0:
                    act.wait_ge(pe_used, r0 * RING + (n - RING + 1))
                act.activation(w_hi[:, s], raw[:, s], ACT.Copy).then_inc(hi_done, 1)

            def chunk_out(to, c, scale_by):
                for b in range(TOK):
                    last = act.activation(to[:, b], proj[:, c % 2, b, :], ACT.Copy,
                                          scale=scale_by[:, b:b + 1])
                last.then_inc(nat_ready, 1)

            def copy_turned(to, bank, n, width):
                act.wait_ge(tr_turned, n)
                act.activation(to, turned[:, bank, 0:width], ACT.Copy).then_inc(tr_copied, 1)

            def x_hi(x_hi_sb, gain, n, base):
                act.wait_ge(xt_turned, base + n + 1)
                for k in range(2):
                    to, of = x_parts(x_hi_sb, n, k, base)
                    last = act.activation(to, of, ACT.Copy, scale=gain[:, 2 * n + k:2 * n + k + 1])
                last.then_inc(xt_hi, 1)

            def sum_squares(c, last_count=None, tiles=(0, 1)):
                if c:
                    act.wait_ge(ssq_done, sq_base[0] + len(tiles) * c)
                for b in tiles:
                    for n, cut in enumerate(HALVES if c == OUT_CHUNKS - 1 else (slice(0, COLS),)):
                        if last_count is not None and n <= b:
                            act.wait_ge(last_h, last_count + b + n + 1)
                        act.activation(squares[:, b, cut],
                                       h[:, b, COLS * c + cut.start:COLS * c + cut.stop],
                                       ACT.Square, accum_out=ssq[:, b, c + n:c + n + 1]
                                       ).then_inc(ssq_done, 1)
                if c == OUT_CHUNKS - 1:
                    sq_base[0] += len(tiles) * SQ_COLS

            sq_base = [0]

            def z_part(c, layer):
                for b in range(TOK):
                    act.activation(e[:, b], proj[:, c % 2, b, :], ACT.Exp,
                                   scale=nrstd[:, layer, b:b + 1]).then_inc(z_exp, 1)

            act.dma_start(sb["first_sb"][:, :], first_in).then_inc(first_landed, 16)
            act.wait_ge(dve_link, 4)
            act.activation(consts[:, 4, :], consts[:, 2, :], ACT.Exp)
            act.wait_ge(first_landed, 16)
            for n in range(2 * OUT_CHUNKS):
                if n in PIECE_BEFORE_X:
                    split(0, PIECE_BEFORE_X[n])
                x_hi(sb["xa_hi"], norm_a_sb, n, 0)
            split(0, POOL_SLOT)
            for c in range(OUT_CHUNKS):
                sum_squares(c, tiles=(0,))
            act.wait_ge(lam_dot, 2)
            act.activation(lam[:, 2:4], lam[:, 0:2], ACT.Exp).then_inc(lam_exp, 1)

            def o_hi_part(n, o_hi, layer):
                act.wait_ge(ot_turned, layer * PIECES + n + 1)
                copy, (hi, of) = nat[:, n % 2, :], o_parts(o_hi, n, layer)
                if n in COPIED_LO:
                    if n - 2 in COPIED_LO:
                        act.wait_ge(copied_lo,
                                    layer * len(COPIED_LO) + COPIED_LO.index(n - 2) + 1)
                    if layer:
                        copy = copy.rearrange("p (k q b) -> p k b q", k=2, b=TOK)
                    act.activation(copy, of if layer else turned[:, n % 2, :], ACT.Copy)
                act.activation(hi, of, ACT.Copy).then_inc(ot_hi, 1)

            def iteration_a(i, last_one):
                for c in range(A_CHUNKS):
                    for j in range(PIECES):
                        if c in (1, 2) and j in (1, 2):
                            to = (q_t, k_t)[c - 1]
                            copy_turned(to[:, 2 * (j - 1):2 * j, :], j - 1,
                                        i * A_TR + (2 * (c - 1) + j), 2 * SEQ)
                        if c == 3 and j == 0:
                            act.wait_ge(max_ready, i + 1)
                            for n in range(4):
                                for b, cut in ((0, slice(0, P)), (1, slice(P, SPAN))):
                                    last = act.activation(
                                        t_a[:, n, cut], t_a[:, n, cut], ACT.Exp, scale=SCALE,
                                        bias=nm[:, b, n:n + 1], accum_out=den[:, b, n:n + 1])
                            last.then_inc(exp_done, 1)
                        if c == 3 and j == 5:
                            for n in range(2):
                                copy_turned(pt_a[:, n, :], n, i * A_TR + 5 + n, SPAN)
                        if c == 3 and j == 7:
                            act.wait_ge(pv_out, i * A_PV + A_PV)
                            for n in range(2):
                                for b in range(TOK):
                                    last = act.activation(
                                        squares[:, b, A_VDIM * n:A_VDIM * (n + 1)],
                                        og[:, b, A_VDIM * n:A_VDIM * (n + 1)], ACT.Square,
                                        accum_out=ssq2[:, n, b:b + 1])
                                    last.then_inc(ssq2_done, 1)
                        if last_one and (c, j) == (A_CHUNKS - 1, FIRST_TURNS_SLOT):
                            for n in range(FIRST_TURNS):
                                o_hi_part(n, sb["oa_hi"], 0)
                        if j == PIECES - 1:
                            act.wait_ge(pe_used, i * (ROUNDS_A * RING) + (c + 1) * PIECES)
                            if c == 0:
                                act.wait_ge(rstd_done, 1)
                            if c < 2:
                                chunk_out(nat, c, rstd[:, 0])
                            elif c == 2:
                                chunk_out(sb["v_a"][:, 0], c, rstd[:, 0])
                            else:
                                z_part(c, 0)
                        split(i * ROUNDS_A, c * PIECES + j + RING)

            with act.Fori(0, A_ITER - 1) as i:
                iteration_a(i, False)
            iteration_a(A_ITER - 1, True)

            def out_projection(o_hi, first_round, layer):
                for c in range(OUT_CHUNKS):
                    for j in range(PIECES):
                        if c == 0:
                            for n in O_TURNS.get(j, ()):
                                o_hi_part(n, o_hi, layer)
                        if c >= 1 and layer == 0 and j in (1, 2):
                            x_hi(sb["xb_hi"], sb["norm_b_sb"], 2 * (c - 1) + j - 1, PIECES)
                        if c >= 1 and j == 3:
                            act.wait_ge(h_ready, layer * (OUT_CHUNKS - 1) + c)
                            sum_squares(c - 1)
                        if first_round * RING + c * PIECES + j + RING < ALL_PIECES:
                            split(first_round, c * PIECES + j + RING)

            out_projection(sb["oa_hi"], OUT_A, 0)
            for n in (6, 7):
                x_hi(sb["xb_hi"], sb["norm_b_sb"], n, PIECES)
            sum_squares(OUT_CHUNKS - 1, 0)

            tr0 = A_ITER * A_TR

            def iteration_b(i, last_one):
                for c in range(B_CHUNKS):
                    for j in range(PIECES):
                        if 1 <= c <= V_B and j in (1, 2):
                            to = (q_t, k_t)[(c - 1) % 2]
                            copy_turned(to[:, 2 * (j - 1):2 * j, :], j - 1,
                                        i * B_TR + (tr0 + 2 * (c - 1) + j), 2 * SEQ)
                        if c == 7 and 1 <= j <= B_HPI:
                            hd = j - 1
                            act.wait_ge(max_ready, i + (A_ITER + 1))
                            for b in range(TOK):
                                last = act.activation(
                                    t_b[:, hd, b], t_b[:, hd, b], ACT.Exp, scale=SCALE,
                                    bias=nm[:, b, hd:hd + 1], accum_out=den[:, b, hd:hd + 1])
                            last.then_inc(exp_done, 1)
                        hd = P_TURNS.get((c, j))
                        if hd is not None:
                            for b in range(TOK):
                                copy_turned(pt_b[:, hd, b], b,
                                            i * B_TR + (tr0 + 4 * NG + TOK * hd + b + 1), B_SPAN)
                        if last_one and (c, j) == (Z_B, FIRST_TURNS_SLOT):
                            for n in range(FIRST_TURNS):
                                o_hi_part(n, sb["ob_hi"], 1)
                        if j == PIECES - 1:
                            act.wait_ge(pe_used,
                                        i * (ROUNDS_B * RING) + (LAYER_B * RING + (c + 1) * PIECES))
                            if c == 0:
                                act.wait_ge(rstd_moved, 4 * 16)
                            if c < V_B:
                                chunk_out(nat, c, rstd[:, 1])
                            elif c < Z_B:
                                chunk_out(sb["v_b"][:, c - V_B], c, rstd[:, 1])
                            else:
                                z_part(c, 1)
                        split(i * ROUNDS_B + LAYER_B, c * PIECES + j + RING)

            with act.Fori(0, B_ITER - 1) as i:
                iteration_b(i, False)
            iteration_b(B_ITER - 1, True)

            out_projection(sb["ob_hi"], OUT_B, 1)
            sum_squares(OUT_CHUNKS - 1, len(LAST_PARTS))
            act.wait_ge(rstd_done, 3)
            act.wait_ge(pre_done, OUT_CHUNKS - 1)
            for c in range(OUT_CHUNKS - 1):
                cut = slice(COLS * c, COLS * (c + 1))
                act.activation(sb["final"][:, 0, cut], sb["final"][:, 0, cut], ACT.Copy,
                               scale=rstd[:, 2, 0:1]).then_inc(final_act, 1)

        @block.vector
        def _(dve):
            own = Links(dve, dve_link)
            link = own.link

            def split(r0, n):
                if n % RING != POOL_SLOT:
                    lo_part(dve, r0, n)

            def x_lo(hi, lo, gain, n, base):
                dve.wait_ge(xt_hi, base + n + 1)
                for k in range(2):
                    to, of = x_parts(lo, n, k, base)
                    last = dve.scalar_tensor_tensor(to, of, gain[:, 2 * n + k:2 * n + k + 1],
                                                    x_parts(hi, n, k, base)[0], ALU.mult,
                                                    ALU.subtract)
                last.then_inc(xt_lo, 1)

            def o_lo_part(n, o_hi, o_lo, layer):
                dve.wait_ge(ot_hi, layer * PIECES + n + 1)
                lo, of = o_parts(o_lo, n, layer)
                dve.tensor_tensor(lo, of, o_parts(o_hi, n, layer)[0], ALU.subtract
                                  ).then_inc(direct_lo, 1)

            def mean_square(count):
                dve.wait_ge(ssq_done, count)
                dve.tensor_reduce(ms[:, 0, 0:TOK], ssq[:, :, :], AX.X, ALU.add
                                  ).then_inc(ms_done, 1)

            def biased(to, n, slope, start, count):
                dve.wait_ge(qk_done, count)
                shape = to.shape
                minus_dist = dist_sb[:, start:start + shape[1] * shape[2]]
                of = score[:, n % 2, 0:shape[1] * shape[2]]
                minus_dist, of = (v.rearrange("p (b n) -> p b n", b=shape[1])
                                  for v in (minus_dist, of))
                dve.scalar_tensor_tensor(to, minus_dist, slope, of, ALU.mult, ALU.add
                                         ).then_inc(t_ready, 1)

            def sigmoid(half, count):
                part = e[:, :, HALVES[half]]
                dve.wait_ge(z_exp, count)
                link(dve.tensor_scalar(part, part, 1.0, None, ALU.add))
                link(dve.reciprocal(part, part))

            def gate(half, c, layer, o_nat, i):
                cut = HALVES[half]
                for b in range(TOK):
                    last = dve.scalar_tensor_tensor(e[:, b, cut], proj[:, c % 2, b, cut],
                                                    rstd[:, layer, b:b + 1], e[:, b, cut],
                                                    ALU.mult, ALU.mult)
                link(last)
                dve.tensor_tensor(o_nat[:, :, bass.ds(i * COLS + cut.start, COLS // 2)],
                                  e[:, :, cut], og[:, :, cut], ALU.mult).then_inc(o_ready, 1)

            for n, value in enumerate((1.0 / D_MODEL, 1.0 / A_VDIM, RMS_EPS, -0.5)):
                dve.memset(consts[:, n, :], value).then_inc(dve_link, 1)
                own.n += 1
            for n in range(2 * OUT_CHUNKS):
                if n in PIECE_BEFORE_X:
                    split(0, PIECE_BEFORE_X[n])
                x_lo(sb["xa_hi"], sb["xa_lo"], norm_a_sb, n, 0)
            for c, cuts in enumerate(((slice(0, COLS),),) * (OUT_CHUNKS - 1) + (HALVES,)):
                for n, cut in enumerate(cuts):
                    part = h[:, 1, COLS * c + cut.start:COLS * c + cut.stop]
                    link(dve.tensor_tensor_reduce(squares[:, 1, cut], part, part, 1.0, 0.0,
                                                  ALU.mult, ALU.add, ssq[:, 1, c + n:c + n + 1]))
            dve.wait_ge(const_landed, 5 * 16)
            lams_sb = sb["lams_sb"]
            for n in range(2):
                dve.tensor_tensor_reduce(sb["lam_prod"][:, n], lams_sb[:, 2 * n],
                                         lams_sb[:, 2 * n + 1], 1.0, 0.0, ALU.mult, ALU.add,
                                         lam[:, n:n + 1]).then_inc(lam_dot, 1)
            dve.tensor_scalar(sb["subln_sb"][:, :], sb["subln_sb"][:, :], 1.0 - LAM_INIT, None,
                              ALU.mult)

            for j in range(PIECES):
                if j == 1:
                    dve.wait_ge(lam_exp, 1)
                    link(dve.tensor_tensor(lam[:, 4:5], lam[:, 3:4], lam[:, 2:3], ALU.subtract))
                    link(dve.tensor_scalar(lam[:, 5:6], lam[:, 4:5], -LAM_INIT, None, ALU.add))
                    mean_square(SQ_COLS)
                if j == 3:
                    dve.wait_ge(rstd_done, 1)
                    link(dve.tensor_scalar(nrstd[:, 0, :], rstd[:, 0, :], -1.0, None, ALU.mult))
                split(0, j + RING)
            before = own.n

            def iteration_a(i, last_one):
                own.base, own.n = i * A_STEPS + before, 0
                for c in range(1, A_CHUNKS + 1):
                    for j in range(PIECES):
                        if c == 2 and j in (4, 6):
                            hd = (j - 4) // 2
                            for n in (j - 4, j - 3):
                                biased(t_a[:, n:n + 1, :], n,
                                       slopes_sb[:, bass.ds(2 * i + hd, 1)], 0,
                                       i * A_QK + (n + 1))
                        if c == 2 and j == 7:
                            dve.wait_ge(t_ready, i * A_QK + A_QK)
                            dve.tensor_reduce(rden[:, 0, :], t_a[:, :, 0:P], AX.X, ALU.max)
                            link(dve.tensor_reduce(rden[:, 1, :], t_a[:, :, P:SPAN], AX.X,
                                                   ALU.max))
                            dve.tensor_scalar(nm[:, :, :], rden[:, :, :], -SCALE, None, ALU.mult
                                              ).then_inc(max_ready, 1)
                        if c == 3 and j == 2:
                            dve.wait_ge(exp_done, i + 1)
                            link(dve.reciprocal(rden[:, :, :], den[:, :, :]))
                            for b, cut in ((0, slice(0, P)), (1, slice(P, SPAN))):
                                for hd in range(2):
                                    last = dve.tensor_scalar(
                                        p_a[:, hd, cut], t_a[:, 2 * hd + 1, cut],
                                        rden[:, b, 2 * hd + 1:2 * hd + 2], lam[:, 5:6], ALU.mult,
                                        ALU.mult)
                            link(last)
                            for b, cut in ((0, slice(0, P)), (1, slice(P, SPAN))):
                                for hd in range(2):
                                    last = dve.scalar_tensor_tensor(
                                        p_a[:, hd, cut], t_a[:, 2 * hd, cut],
                                        rden[:, b, 2 * hd:2 * hd + 1], p_a[:, hd, cut], ALU.mult,
                                        ALU.add)
                            last.then_inc(p_ready, 1)
                        if c == 3 and j == 6:
                            for hd in range(2):
                                dve.wait_ge(pv_done, i * A_PV + (hd + 1))
                                dve.tensor_copy(
                                    og[:, :, A_VDIM * hd:A_VDIM * (hd + 1)],
                                    score[:, hd, :].rearrange("p (b n) -> p b n", b=TOK)
                                ).then_inc(pv_out, 1)
                        if last_one and (c, j) == (A_CHUNKS - 1, FIRST_TURNS_SLOT):
                            for n in range(FIRST_TURNS):
                                o_lo_part(n, sb["oa_hi"], sb["oa_lo"], 0)
                        if last_one and c == A_CHUNKS:
                            for n in O_TURNS.get(j, ()):
                                if n in DIRECT_LO:
                                    o_lo_part(n, sb["oa_hi"], sb["oa_lo"], 0)
                        if c == A_CHUNKS and j == 0:
                            dve.wait_ge(rstd2_done, i + 1)
                            for hd in range(2):
                                for b in range(TOK):
                                    part = og[:, b, A_VDIM * hd:A_VDIM * (hd + 1)]
                                    last = dve.scalar_tensor_tensor(
                                        part, part, rstd2[:, hd, b:b + 1], sb["subln_sb"][:, :],
                                        ALU.mult, ALU.mult)
                            link(last)
                        step = j if last_one else j - 1
                        if c == A_CHUNKS and step in (0, 2):
                            sigmoid(step // 2, i * TOK + TOK)
                        if c == A_CHUNKS and step in (1, 3):
                            gate(step // 2, A_CHUNKS - 1, 0, sb["oa_nat"], i)
                        split(i * ROUNDS_A, c * PIECES + j + RING)
                assert own.n == A_STEPS, own.n

            with dve.Fori(0, A_ITER - 1) as i:
                iteration_a(i, False)
            iteration_a(A_ITER - 1, True)
            own.base, own.n = 0, before + A_ITER * A_STEPS

            def out_projection(first_round, layer):
                for c in range(OUT_CHUNKS):
                    cut = slice(COLS * c, COLS * (c + 1))
                    for j in range(PIECES):
                        if c >= 1 and layer == 0 and j in (1, 2):
                            x_lo(sb["xb_hi"], sb["xb_lo"], sb["norm_b_sb"], 2 * (c - 1) + j - 1,
                                 PIECES)
                        if j == PIECES - 1 and c < OUT_CHUNKS - 1:
                            dve.wait_ge(pe_used, first_round * RING + (c + 1) * PIECES)
                            dve.tensor_tensor(h[:, :, cut], h[:, :, cut], proj[:, c % 2, :, :],
                                              ALU.add).then_inc(h_ready, 1)
                        if c >= 1 and first_round * RING + c * PIECES + j + RING < ALL_PIECES:
                            split(first_round, c * PIECES + j + RING)
                for n, (b, part) in enumerate(LAST_PARTS):
                    if n == 0:
                        dve.wait_ge(tile_done, layer + 1)
                    if n == 1:
                        dve.wait_ge(pe_used, (first_round + ROUNDS_OUT) * RING)
                    to = h[:, b, cut.start + part.start:cut.start + part.stop]
                    dve.tensor_tensor(to, to, proj[:, (OUT_CHUNKS - 1) % 2, b, part], ALU.add
                                      ).then_inc(last_h, 1)
                    if n == 0 and layer == 1:
                        pre_last(0)

            def pre_last(b):
                dve.wait_ge(last_h, len(LAST_PARTS) + (1, len(LAST_PARTS))[b])
                cut = slice(D_MODEL - COLS, D_MODEL)
                dve.tensor_tensor(sb["final"][:, b, cut], h[:, b, cut], sb["normf_sb"][:, cut],
                                  ALU.mult).then_inc(last_pre, 1)

            out_projection(OUT_A, 0)
            for n in (6, 7):
                x_lo(sb["xb_hi"], sb["xb_lo"], sb["norm_b_sb"], n, PIECES)
            for j in range(PIECES):
                if j == 0:
                    mean_square(SQ_COLS + SQ_NORM)
                if j == 4:
                    dve.wait_ge(rstd_moved, 4 * 16)
                    link(dve.tensor_scalar(nrstd[:, 1, :], rstd[:, 1, :], -1.0, None, ALU.mult))
                split(LAYER_B, j + RING)

            before = own.n
            qk0, pv0 = A_ITER * A_QK, A_ITER * A_PV

            def iteration_b(i, last_one):
                own.base, own.n = i * B_STEPS + before, 0
                for c in range(1, B_CHUNKS + 1):
                    for j in range(PIECES):
                        if c in (2, 4, 6) and j in (4, 6):
                            g = c // 2 - 1
                            for hd in (j - 4, j - 3):
                                biased(t_b[:, hd, :, B_STARTS[g]:B_STARTS[g] + B_WIDTHS[g]], hd,
                                       slopes_sb[:, bass.ds(B_HPI * i + (A_HEADS + hd), 1)],
                                       DIST_STARTS[g], i * B_QK + (qk0 + B_HPI * g + hd + 1))
                        if (c, j) in ((6, 7), (7, 0)):
                            two = slice(2 * (c - 6), 2 * (c - 6) + 2)
                            dve.wait_ge(t_ready, i * B_QK + (qk0 + B_QK))
                            link(dve.tensor_reduce(rden[:, :, two].rearrange("p b h -> p h b"),
                                                   t_b[:, two], AX.X, ALU.max))
                        if c == 7 and j == 0:
                            dve.tensor_scalar(nm[:, :, :], rden[:, :, :], -SCALE, None, ALU.mult
                                              ).then_inc(max_ready, 1)
                        if c == Z_B and j == 0:
                            dve.wait_ge(exp_done, i * B_HPI + (A_ITER + B_HPI))
                            link(dve.reciprocal(rden[:, :, :], den[:, :, :]))
                        if c == Z_B and 1 <= j <= B_HPI:
                            hd = j - 1
                            dve.wait_ge(pv_done, i * B_PV + (pv0 + hd + 1))
                            for b in range(TOK):
                                last = dve.tensor_scalar(
                                    og[:, b, HEAD * hd:HEAD * (hd + 1)],
                                    score[:, hd % 2, P * b:P * (b + 1)], rden[:, b, hd:hd + 1],
                                    None, ALU.mult)
                            last.then_inc(pv_out, 1)
                        if last_one and (c, j) == (Z_B, FIRST_TURNS_SLOT):
                            for n in range(FIRST_TURNS):
                                o_lo_part(n, sb["ob_hi"], sb["ob_lo"], 1)
                        if last_one and c == B_CHUNKS:
                            for n in O_TURNS.get(j, ()):
                                if n in DIRECT_LO:
                                    o_lo_part(n, sb["ob_hi"], sb["ob_lo"], 1)
                        if c == B_CHUNKS and j in (0, 2):
                            sigmoid(j // 2, i * TOK + (A_ITER * TOK + TOK))
                        if c == B_CHUNKS and j in (1, 3):
                            if j == 1:
                                dve.wait_ge(pv_out, i * B_PV + (pv0 + B_PV))
                            gate(j // 2, Z_B, 1, sb["ob_nat"], i)
                        split(i * ROUNDS_B + LAYER_B, c * PIECES + j + RING)
                assert own.n == B_STEPS, own.n

            with dve.Fori(0, B_ITER - 1) as i:
                iteration_b(i, False)
            iteration_b(B_ITER - 1, True)
            own.base, own.n = 0, before + B_ITER * B_STEPS

            out_projection(OUT_B, 1)
            mean_square(SQ_COLS + 2 * SQ_NORM)
            pre_last(1)
            dve.wait_ge(rstd_done, 3)
            dve.wait_ge(pre_done, OUT_CHUNKS - 1)
            for b, c in DVE_STORES:
                if c == OUT_CHUNKS - 1:
                    dve.wait_ge(last_pre, TOK)
                cut = slice(COLS * c, COLS * (c + 1))
                dve.tensor_scalar(sb["final"][:, b, cut], sb["final"][:, b, cut],
                                  rstd[:, 2, b:b + 1], None, ALU.mult).then_inc(final_dve, 1)

        @block.gpsimd
        def _(pool):
            own = Links(pool, pool_link)

            def rsqrt(to, of, tmp, norm, done):
                wide = tmp.shape[1]
                own.link(pool.tensor_tensor(tmp, of, consts[:, norm, 0:wide], ALU.mult))
                own.link(pool.tensor_tensor(tmp, tmp, consts[:, 2, 0:wide], ALU.add))
                pool.tensor_tensor(to, tmp, consts[:, 3, 0:wide], ALU.pow).then_inc(done, 1)

            def token_norm(n):
                pool.wait_ge(ms_done, n + 1)
                to = rstd_nat[:, :] if n == 1 else rstd[:, n, :]
                rsqrt(to, ms[:, 0, 0:TOK], ms[:, 1, 0:TOK], 0, rstd_done)

            def split(r0, n):
                if n % RING == POOL_SLOT and r0 * RING + n < ALL_PIECES:
                    lo_part(pool, r0, n)

            def o_lo_part(o_hi, o_lo, n, layer):
                pool.wait_ge(ot_hi, layer * PIECES + n + 1)
                pool.tensor_tensor(o_lo[:, 2 * n:2 * n + 2, :],
                                   nat[:, n % 2, :].rearrange("p (k s) -> p k s", k=2),
                                   o_hi[:, 2 * n:2 * n + 2, :], ALU.subtract).then_inc(copied_lo, 1)

            def out_projection(o_hi, o_lo, first_round, layer):
                for c in range(OUT_CHUNKS):
                    for j in range(PIECES):
                        if c == 0:
                            for n in O_TURNS.get(j, ()):
                                if n in COPIED_LO:
                                    o_lo_part(o_hi, o_lo, n, layer)
                        if c >= 1 and j == 1 and layer == 1:
                            pool.wait_ge(h_ready, OUT_CHUNKS - 1 + c)
                            cut = slice(COLS * (c - 1), COLS * c)
                            for b in range(TOK):
                                last = pool.tensor_tensor(sb["final"][:, b, cut], h[:, b, cut],
                                                          sb["normf_sb"][:, cut], ALU.mult)
                            last.then_inc(pre_done, 1)
                        split(first_round, c * PIECES + j + RING)

            pool.wait_ge(dve_link, 4)
            split(0, POOL_SLOT)
            token_norm(0)
            before = own.n
            with pool.Fori(0, A_ITER) as i:
                own.base, own.n = i * 2 + before, 0
                for r in range(1, ROUNDS_A + 1):
                    if r == ROUNDS_A:
                        pool.wait_ge(ssq2_done, i * 4 + 4)
                        rsqrt(rstd2[:, :, :].rearrange("p a b -> p (a b)"),
                              ssq2[:, :, :].rearrange("p a b -> p (a b)"), ms[:, 1, 4:8], 1,
                              rstd2_done)
                    lo_part(pool, i * ROUNDS_A, r * RING + POOL_SLOT)
            own.base, own.n = 0, before + 2 * A_ITER
            out_projection(sb["oa_hi"], sb["oa_lo"], OUT_A, 0)
            token_norm(1)
            pool.wait_ge(rstd_done, 2)
            for b in range(TOK):
                for k in range(TOK):
                    rows = slice(P // 2 * k, P // 2 * (k + 1))
                    pool.dma_start(rstd[rows, 1, b:b + 1], rstd_nat[b:P:TOK, k:k + 1]
                                   ).then_inc(rstd_moved, 16)
            with pool.Fori(0, B_ITER) as i:
                for r in range(1, ROUNDS_B + 1):
                    lo_part(pool, i * ROUNDS_B + LAYER_B, r * RING + POOL_SLOT)
            pool.wait_ge(normf_landed, 16)
            out_projection(sb["ob_hi"], sb["ob_lo"], OUT_B, 1)
            token_norm(2)


def distances():
    def part(query, key, dilation, window):
        far = query[:, None] - key[None, :]
        seen = (far >= 0) & (far % dilation == 0) & (far <= window)
        return np.where(seen, -far.astype(np.float32), np.float32(MASKED))

    place = np.arange(P)
    parts = [part(place, place, 1, SEQ), part(P + place, np.arange(SEQ), 1, SEQ)]
    tokens = [TOK * place + b for b in range(TOK)]
    for (window, dilation), width in zip(B_GROUPS, B_WIDTHS):
        for b in range(TOK):
            keys = np.concatenate(tokens) if width == SEQ else tokens[b]
            parts.append(part(tokens[b], keys, dilation, window))
    return np.concatenate(parts, 1).astype(np.float32)


def slope_table():
    slopes = [2.0 ** (-8.0 * (np.arange(n) + 1.0) / n) / SCALE for n in (A_HEADS, B_HEADS)]
    return np.tile(np.concatenate(slopes).astype(np.float32)[None, :], (P, 1))


def kernel(x, norm_a, w_in_a, lam_q1, lam_k1, lam_q2, lam_k2, subln_a, w_out_a, norm_b, w_in_b,
           w_out_b, norm_f):
    import concourse.bacc as bacc
    from concourse.bass_utils import run_bass_kernel_spmd

    def rows(v, n):
        return np.ascontiguousarray(np.broadcast_to(np.asarray(v).reshape(1, n), (P, n)))

    def by_tile(v):
        return np.ascontiguousarray(np.asarray(v).reshape(KT, P).T)

    arrays = {
        "x_dram": np.asarray(x)[0],
        "w_in_a_dram": np.asarray(w_in_a)[0],
        "w_out_a_dram": np.asarray(w_out_a)[0],
        "w_in_b_dram": np.asarray(w_in_b)[0],
        "w_out_b_dram": np.asarray(w_out_b)[0],
        "first_dram": np.concatenate([np.eye(P, dtype=np.float32), by_tile(norm_a)], 1),
        "norm_b_dram": by_tile(norm_b),
        "norm_f_dram": rows(norm_f, D_MODEL),
        "subln_dram": rows(subln_a, A_VDIM),
        "lams_dram": np.concatenate([rows(v, HEAD) for v in (lam_q1, lam_k1, lam_q2, lam_k2)], 1),
        "dist_dram": distances(),
        "slopes_dram": slope_table(),
    }
    arrays = {k: np.ascontiguousarray(v) for k, v in arrays.items()}
    nc = bacc.Bacc("TRN2", target_bir_lowering=False, num_devices=1)
    ins = [nc.dram_tensor(k, v.shape, mybir.dt.from_np(v.dtype), kind="ExternalInput").ap()
           for k, v in arrays.items()]
    out = nc.dram_tensor("out_dram", (SEQ, D_MODEL), F32, kind="ExternalOutput").ap()
    hybrid(nc, *ins, out)
    got = run_bass_kernel_spmd(nc, [arrays], core_ids=[0])
    return got.results[0]["out_dram"].reshape(1, SEQ, D_MODEL)
```
